# Optimizing a Trainium2 kernel written in Bass

```python
import math
import jax, jax.numpy as jnp
from jax import lax
import numpy as np

D_MODEL = 1024
BATCH = 1
SEQ = 1024
DEPTH = 1

N_META = 16
MIX_WIDTH = D_MODEL
ATTN_WIDTH = MIX_WIDTH // 2
CONV_WIDTH = MIX_WIDTH - ATTN_WIDTH
N_ATTN_HEADS = 4
DIFF_HEAD_DIM = ATTN_WIDTH // (2 * N_ATTN_HEADS)
V_HEAD_DIM = 2 * DIFF_HEAD_DIM
CONV_KERNEL = 31
N_CONV_GROUPS = 8
CONV_GROUP_DIM = CONV_WIDTH // N_CONV_GROUPS
Q_BLOCK = 128
PEER_HEADS = 8
PEER_KEYS = 128
PEER_EXPERTS = PEER_KEYS * PEER_KEYS
PEER_QUERY_DIM = 256
PEER_HALF = PEER_QUERY_DIM // 2
PEER_TOPK = 16
PEER_CHUNK = 128
NORM_EPS = 1e-6
IN_COLS = 3 * ATTN_WIDTH + 2 * CONV_WIDTH

kernel_name = "hymba_diffattn_conformer_peer_block"

def lambda_init_for(layer):
    return 0.8 - 0.6 * math.exp(-0.3 * layer)

def alibi_slopes(n_heads):
    return jnp.asarray(np.array([2.0 ** (-8.0 * (i + 1) / n_heads) for i in range(n_heads)], dtype=np.float32))

def rms_norm(x, g):
    xf = x.astype(jnp.float32)
    y = xf * lax.rsqrt(jnp.mean(xf * xf, axis=-1, keepdims=True) + NORM_EPS)
    return (y * g.astype(jnp.float32)).astype(x.dtype)

def diff_attention(q, k, v, lam, lam_init, sub_g, slopes):
    B, Lp = q.shape[0], q.shape[1]
    n_blocks = Lp // Q_BLOCK
    scale = DIFF_HEAD_DIM ** -0.5
    k_pos = jnp.arange(Lp)

    def block(i):
        start = i * Q_BLOCK
        qb = lax.dynamic_slice_in_dim(q, start, Q_BLOCK, axis=1)
        s = jnp.einsum('bqhcd,bkhcd->bhcqk', qb, k).astype(jnp.float32) * scale
        dist = (start + jnp.arange(Q_BLOCK))[:, None] - k_pos[None, :]
        bias = jnp.where(dist[None] >= 0,
                         -slopes[:, None, None] * dist[None].astype(jnp.float32),
                         -jnp.inf)
        p = jax.nn.softmax(s + bias[None, :, None], axis=-1)
        a = p[:, :, 0] - lam * p[:, :, 1]
        return jnp.einsum('bhqk,bkhd->bqhd', a.astype(v.dtype), v)

    out = lax.map(block, jnp.arange(n_blocks))
    out = jnp.moveaxis(out, 0, 1).reshape(B, Lp, N_ATTN_HEADS, V_HEAD_DIM)
    out = rms_norm(out, sub_g) * (1.0 - lam_init)
    return out.reshape(B, Lp, ATTN_WIDTH)

def conformer_conv(a, g, conv_w, conv_b, gn_g, gn_b):
    B, Lp, C = a.shape
    u = a * jax.nn.sigmoid(g)
    y = lax.conv_general_dilated(u, conv_w[:, None, :], window_strides=(1,),
                                 padding=[(CONV_KERNEL - 1, 0)],
                                 dimension_numbers=('NWC', 'WIO', 'NWC'),
                                 feature_group_count=C) + conv_b
    yg = y.reshape(B, Lp, N_CONV_GROUPS, CONV_GROUP_DIM).astype(jnp.float32)
    mu = jnp.mean(yg, axis=-1, keepdims=True)
    var = jnp.mean(jnp.square(yg - mu), axis=-1, keepdims=True)
    yn = ((yg - mu) * lax.rsqrt(var + NORM_EPS)).reshape(B, Lp, C)
    yn = yn * gn_g.astype(jnp.float32) + gn_b.astype(jnp.float32)
    return jax.nn.silu(yn).astype(a.dtype)

def peer_ffn(xn, wq, subkeys, u_tab, v_tab):
    T = xn.shape[0]
    xc = xn.reshape(T // PEER_CHUNK, PEER_CHUNK, D_MODEL)

    def chunk(xt):
        q = (xt @ wq).reshape(PEER_CHUNK, PEER_HEADS, 2, PEER_HALF)
        s = jnp.einsum('thpk,hpnk->thpn', q, subkeys).astype(jnp.float32)
        s_top, i_top = lax.top_k(s, PEER_TOPK)
        cand = s_top[:, :, 0, :, None] + s_top[:, :, 1, None, :]
        cand = cand.reshape(PEER_CHUNK, PEER_HEADS, PEER_TOPK * PEER_TOPK)
        c_top, c_idx = lax.top_k(cand, PEER_TOPK)
        i1 = jnp.take_along_axis(i_top[:, :, 0, :], c_idx // PEER_TOPK, axis=-1)
        i2 = jnp.take_along_axis(i_top[:, :, 1, :], c_idx % PEER_TOPK, axis=-1)
        e = i1 * PEER_KEYS + i2
        gate = jax.nn.softmax(c_top, axis=-1)
        act = jax.nn.gelu(jnp.einsum('thkd,td->thk', u_tab[e], xt).astype(jnp.float32), approximate=False)
        w = (gate * act).astype(xt.dtype)
        return jnp.einsum('thk,thkd->td', w, v_tab[e])

    return lax.map(chunk, xc).reshape(T, D_MODEL)

def setup_inputs(seed: int = 0) -> dict:
    key = jax.random.key(seed)
    ks = jax.random.split(key, 24)
    f32 = jnp.float32
    nrm = lambda k, shape, s: jax.random.normal(k, shape, f32) * s
    return {
        "x": nrm(ks[0], (BATCH, SEQ, D_MODEL), 1.0),
        "meta_tokens": nrm(ks[1], (N_META, D_MODEL), 1.0),
        "norm1_g": 1.0 + nrm(ks[2], (DEPTH, D_MODEL), 0.02),
        "w_in": nrm(ks[3], (DEPTH, D_MODEL, IN_COLS), D_MODEL ** -0.5),
        "lambda_q1": nrm(ks[4], (DEPTH, DIFF_HEAD_DIM), 0.1),
        "lambda_k1": nrm(ks[5], (DEPTH, DIFF_HEAD_DIM), 0.1),
        "lambda_q2": nrm(ks[6], (DEPTH, DIFF_HEAD_DIM), 0.1),
        "lambda_k2": nrm(ks[7], (DEPTH, DIFF_HEAD_DIM), 0.1),
        "attn_subln_g": 1.0 + nrm(ks[8], (DEPTH, V_HEAD_DIM), 0.02),
        "conv_w": nrm(ks[9], (DEPTH, CONV_KERNEL, CONV_WIDTH), CONV_KERNEL ** -0.5),
        "conv_b": nrm(ks[10], (DEPTH, CONV_WIDTH), 0.02),
        "conv_norm_g": 1.0 + nrm(ks[11], (DEPTH, CONV_WIDTH), 0.02),
        "conv_norm_b": nrm(ks[12], (DEPTH, CONV_WIDTH), 0.02),
        "w_out": nrm(ks[13], (DEPTH, MIX_WIDTH, D_MODEL), MIX_WIDTH ** -0.5),
        "norm2_g": 1.0 + nrm(ks[14], (DEPTH, D_MODEL), 0.02),
        "peer_wq": nrm(ks[15], (DEPTH, D_MODEL, PEER_HEADS * PEER_QUERY_DIM), D_MODEL ** -0.5),
        "peer_subkeys": nrm(ks[16], (DEPTH, PEER_HEADS, 2, PEER_KEYS, PEER_HALF), PEER_HALF ** -0.5),
        "peer_u": nrm(ks[17], (DEPTH, PEER_EXPERTS, D_MODEL), D_MODEL ** -0.5),
        "peer_v": nrm(ks[18], (DEPTH, PEER_EXPERTS, D_MODEL), PEER_HEADS ** -0.5),
        "final_norm_g": 1.0 + nrm(ks[19], (D_MODEL,), 0.02),
    }

def reference(x, meta_tokens, norm1_g, w_in, lambda_q1, lambda_k1, lambda_q2, lambda_k2,
              attn_subln_g, conv_w, conv_b, conv_norm_g, conv_norm_b, w_out, norm2_g,
              peer_wq, peer_subkeys, peer_u, peer_v, final_norm_g):
    B, S = x.shape[0], x.shape[1]
    L = N_META + S
    Lp = ((L + Q_BLOCK - 1) // Q_BLOCK) * Q_BLOCK
    meta = jnp.broadcast_to(meta_tokens[None].astype(x.dtype), (B, N_META, D_MODEL))
    h = jnp.concatenate([meta, x], axis=1)
    h = jnp.pad(h, ((0, 0), (0, Lp - L), (0, 0)))
    slopes = alibi_slopes(N_ATTN_HEADS)

    for l in range(DEPTH):
        lam_init = lambda_init_for(l)
        xn = rms_norm(h, norm1_g[l])
        proj = xn @ w_in[l]
        q, k, v, ga, gg = jnp.split(
            proj, [ATTN_WIDTH, 2 * ATTN_WIDTH, 3 * ATTN_WIDTH, 3 * ATTN_WIDTH + CONV_WIDTH], axis=-1)
        q = q.reshape(B, Lp, N_ATTN_HEADS, 2, DIFF_HEAD_DIM)
        k = k.reshape(B, Lp, N_ATTN_HEADS, 2, DIFF_HEAD_DIM)
        v = v.reshape(B, Lp, N_ATTN_HEADS, V_HEAD_DIM)
        lam = (jnp.exp(jnp.sum(lambda_q1[l].astype(jnp.float32) * lambda_k1[l].astype(jnp.float32)))
               - jnp.exp(jnp.sum(lambda_q2[l].astype(jnp.float32) * lambda_k2[l].astype(jnp.float32)))
               + lam_init)
        attn_out = diff_attention(q, k, v, lam, lam_init, attn_subln_g[l], slopes)
        conv_out = conformer_conv(ga, gg, conv_w[l], conv_b[l], conv_norm_g[l], conv_norm_b[l])
        h = h + jnp.concatenate([attn_out, conv_out], axis=-1) @ w_out[l]

        xn2 = rms_norm(h, norm2_g[l])
        ffn = peer_ffn(xn2.reshape(B * Lp, D_MODEL), peer_wq[l], peer_subkeys[l], peer_u[l], peer_v[l])
        h = h + ffn.reshape(B, Lp, D_MODEL)

    h = rms_norm(h, final_norm_g)
    return h[:, N_META:N_META + S]


_drawn_inputs = setup_inputs


def setup_inputs(seed=0):
    import zlib

    import numpy as np

    out = dict(_drawn_inputs(seed))
    spreads = {}
    factors = {'attn_subln_g': 31.905,
     'conv_norm_g': 37.144,
     'conv_norm_b': 37.624,
     'final_norm_g': 22.688,
     'norm2_g': 18.248}
    for name, (base, spread) in spreads.items():
        noise = np.random.default_rng([zlib.crc32(name.encode()), seed]).standard_normal(out[name].shape)
        drawn = base * np.exp(spread * noise) if base else spread * noise
        out[name] = __import__('jax').numpy.asarray(drawn.astype(out[name].dtype))
    for name, factor in factors.items():
        out[name] = (out[name] * factor).astype(out[name].dtype)
    return out
```

```python
import math
from contextlib import ExitStack

import concourse.bass as bass
from concourse import mybir

F32 = mybir.dt.float32
U32 = mybir.dt.uint32
I32 = mybir.dt.int32
ALU = mybir.AluOpType
ACT = mybir.ActivationFunctionType
AX = mybir.AxisListType

P = 128
D = 1024
KC = D // P
SEQ = 1024
NT = SEQ // P
META = 16
POS = META + SEQ
HEADS = 4
COMP = 64
AW = HEADS * 2 * COMP
CG = 4
TAPS = 31
GROUP = 64
IN_COLS = 3 * AW + 2 * CG * P
EPS = 1e-6
LAM_INIT = 0.8 - 0.6 * math.exp(0.0)
SCALE = COMP ** -0.5
SLOPE0 = 2.0 ** (-8.0 / HEADS)
MASKED = -1.0e30
PH = 8
KEYS = 128
TOPK = 16
QH = 128
CAND = TOPK * TOPK
RING = 8
DIAGS = 4
SEGS = [(0, 352), (352, 352), (704, 336)]
NEG = -3.0e38


def conv_params_cols():
    return TAPS + 3


def mixer_phase(nc, x, meta, g1, w_in, lam_vecs, sub_g, conv_p, mix_dram):
    ctx = ExitStack()
    with ctx:
        def sb(name, shape, dt=F32):
            return ctx.enter_context(nc.sbuf_tensor(name, shape, dt))

        def pb(name, shape):
            return ctx.enter_context(nc.psum_tensor(name, shape, F32))

        def sem(name):
            return ctx.enter_context(nc.semaphore(name))

        ident = sb("identA", [P, P])
        group_mean = sb("group_mean", [P, P])
        g1_cols = sb("g1_cols", [P, KC])
        sub_gain = sb("sub_gain", [P, 1])
        eps_col = sb("eps_col", [P, 1])
        lam_in = sb("lam_in", [P, 4, COMP])
        lam_s = sb("lam_s", [P, 4])
        dist_i = sb("dist_i", [P, POS], I32)
        bias = sb("bias", [P, POS])
        x_in = sb("x_in", [P, 2, D])
        xn = sb("xn", [P, 2, D])
        ssum = sb("ssum", [P, 2])
        rstd = sb("rstd", [P, 2])
        xnT_tile = sb("xnT_tile", [P, 2, KC, P])
        xnT = sb("xnT", [P, KC, POS])
        wv = sb("wv", [P, KC, AW])
        v_all = sb("v_all", [P, NT, AW])
        v_meta = sb("v_meta", [META, AW])
        w_slot = sb("w_slot", [P, 2, KC, P])
        cpar = sb("cpar", [P, CG, conv_params_cols()])
        gate_sig = sb("gate_sig", [P, POS])
        u_pad = sb("u_pad", [P, TAPS - 1 + POS])
        y = sb("y", [P, SEQ])
        yc = sb("yc", [P, SEQ])
        ysq = sb("ysq", [P, SEQ])
        ystd = sb("ystd", [P, SEQ])
        conv_out = sb("conv_out", [P, SEQ])
        q_next = sb("q_next", [P, POS])
        k_next = sb("k_next", [P, POS])
        qT = sb("qT", [P, SEQ])
        kT = sb("kT", [P, POS])
        z = sb("z", [P, 2, 2, POS])
        zmax = sb("zmax", [P, 2, 2, 3])
        nmax = sb("nmax", [P, 2, 2])
        zsum = sb("zsum", [P, 2, 2])
        zinv = sb("zinv", [P, 2, 2])
        aT = sb("aT", [P, 2, 4 * P])
        aT_meta = sb("aT_meta", [META, P])
        o_all = sb("o_all", [P, NT, P])
        o_sq = sb("o_sq", [P, NT, P])
        o_ss = sb("o_ss", [P, NT])
        o_rs = sb("o_rs", [P, NT])
        head_out = sb("head_out", [P, SEQ])

        banks = [pb(f"bankA{i}", [P, 512]) for i in range(8)]

        s_const = sem("a_const")
        s_gate = sem("a_gate")
        s_par = sem("a_par")
        s_lam = sem("a_lam")
        s_x = [sem("a_x0"), sem("a_x1")]
        s_ss = sem("a_ss")
        s_var = sem("a_var")
        s_std = sem("a_std")
        s_rstd = sem("a_rstd")
        s_xn = sem("a_xn")
        s_xT = sem("a_xT")
        s_xTs = sem("a_xTs")
        s_xTall = sem("a_xTall")
        s_wv = sem("a_wv")
        s_v = sem("a_v")
        s_vs = sem("a_vs")
        s_w = [sem("a_w0"), sem("a_w1")]
        s_gproj = sem("a_gproj")
        s_aproj = sem("a_aproj")
        s_sig = sem("a_sig")
        s_u = sem("a_u")
        s_tap = sem("a_tap")
        s_mean = sem("a_mean")
        s_yc = sem("a_yc")
        s_ysq = sem("a_ysq")
        s_yvar = sem("a_yvar")
        s_ystd = sem("a_ystd")
        s_yrec = sem("a_yrec")
        s_yn = sem("a_yn")
        s_cout = sem("a_cout")
        s_cst = sem("a_cst")
        s_qk = sem("a_qk")
        s_qks = sem("a_qks")
        s_cur = sem("a_cur")
        s_sc = sem("a_sc")
        s_z = sem("a_z")
        s_nm = sem("a_nm")
        s_exp = sem("a_exp")
        s_inv = sem("a_inv")
        s_t1 = sem("a_t1")
        s_a = sem("a_a")
        s_mt = sem("a_mt")
        s_mts = sem("a_mts")
        s_at = sem("a_at")
        s_ats = sem("a_ats")
        s_pv = sem("a_pv")
        s_o = sem("a_o")
        s_fin = sem("a_fin")
        s_ostd = sem("a_ostd")
        s_oT = sem("a_oT")
        s_ho = sem("a_ho")
        s_hst = sem("a_hst")
        s_bias = sem("a_bias")

        block = ctx.enter_context(nc.Block())

        CHUNKS = [-(-(META + P * (i + 1)) // 512) for i in range(NT)]
        GROUPS = [-(-(i + 1) // 4) for i in range(NT)]
        SC_H = 2 * sum(CHUNKS)
        GR_H = sum(GROUPS)
        assert SC_H % 2 == 0 and GR_H % 2 == 0

        def chunk(i, n):
            nk = META + P * (i + 1)
            w = -(-nk // CHUNKS[i] // 8) * 8
            return n * w, min(nk, (n + 1) * w)

        def sc_before(i, c):
            return 2 * sum(CHUNKS[:i]) + c * CHUNKS[i]

        def gr_before(i):
            return sum(GROUPS[:i])

        w_in_v = w_in.rearrange("(k p) n -> p k n", p=P)
        x_banks = [banks[0:2], banks[2:4]]
        NM = NT + 1

        def over_tiles(eng, step):
            step(0, 1)
            step(1, 0)
            with eng.Fori(0, (NM - 3) // 2) as j:
                step(2 * j + 2, 1)
                step(2 * j + 3, 0)
            step(NM - 1, 1)

        def reused(m):
            return not (isinstance(m, int) and m < 2)

        def rows(m):
            return META if isinstance(m, int) and m == 0 else P

        @block.gpsimd
        def _(pool):
            pool.memset(ident[:], 0.0).then_inc(s_const, 1)
            pool.memset(group_mean[:], 1.0 / GROUP).then_inc(s_const, 1)
            pool.iota(dist_i[:], [[1, POS]], base=-(META + SEQ - P), channel_multiplier=-1).then_inc(s_const, 1)
            pool.memset(eps_col[:], EPS).then_inc(s_const, 1)
            pool.memset(u_pad[:, 0:TAPS - 1], 0.0).then_inc(s_const, 1)
            pool.wait_ge(s_const, 5)
            pool.affine_select(out=ident[:], in_=ident[:], compare_op=ALU.not_equal, fill=1.0, base=0,
                               pattern=[[-1, P]], channel_multiplier=1).then_inc(s_const, 1)
            pool.affine_select(out=group_mean[:, 0:GROUP], in_=group_mean[:, 0:GROUP], compare_op=ALU.is_ge,
                               fill=0.0, base=GROUP - 1, pattern=[[0, GROUP]],
                               channel_multiplier=-1).then_inc(s_const, 1)
            pool.affine_select(out=group_mean[:, GROUP:P], in_=group_mean[:, GROUP:P], compare_op=ALU.is_ge,
                               fill=0.0, base=-GROUP, pattern=[[0, GROUP]],
                               channel_multiplier=1).then_inc(s_const, 1)
            pool.tensor_copy(bias[:], dist_i[:]).then_inc(s_const, 1)
            pool.wait_ge(s_const, 9)
            pool.affine_select(out=bias[:], in_=bias[:], compare_op=ALU.is_ge, fill=MASKED,
                               base=META + SEQ - P, pattern=[[-1, POS]], channel_multiplier=1).then_inc(s_const, 1)

            def whole(m, slot):
                pool.wait_ge(s_xTs, m + 1)
                pool.sem_inc(s_gate, 1)
                dst = xnT[:, :, 0:META] if rows(m) == META else xnT[:, :, bass.ds((m - 1) * P + META, P)]
                pool.tensor_copy(dst, xnT_tile[:, slot, :, 0:rows(m)]).then_inc(s_xTall, 1)

            over_tiles(pool, whole)

            def current(h):
                pool.wait_ge(s_qks, 6 * (h + 1))
                pool.sem_inc(s_gate, 1)
                pool.tensor_copy(qT[:], q_next[:, META:POS]).then_inc(s_cur, 1)
                pool.tensor_copy(kT[:], k_next[:]).then_inc(s_cur, 1)

            def head(h, last):
                for i in range(NT):
                    nk = META + P * (i + 1)
                    pool.wait_ge(s_inv, 2 * (NT * h + i + 1))
                    pool.sem_inc(s_gate, 1)
                    pool.tensor_scalar(z[:, i % 2, 1, 0:nk], z[:, i % 2, 1, 0:nk], zinv[:, i % 2, 1:2], None,
                                       ALU.mult).then_inc(s_t1, 1)
                if not last:
                    pool.wait_ge(s_sc, SC_H * (h + 1))
                    pool.sem_inc(s_gate, 1)
                    pool.wait_ge(s_ho, 2 * (h + 1))
                    pool.sem_inc(s_gate, 1)
                    current(h + 1)

            current(0)
            with pool.Fori(0, HEADS - 1) as h:
                head(h, False)
            head(HEADS - 1, True)

        @block.sync
        def _(sp):
            with nc.allow_non_contiguous_dma(reason="small parameter columns"):
                sp.dma_start(g1_cols[:], g1.rearrange("(k p) -> p k", p=P)).then_inc(s_par, 16)
                sp.dma_start(sub_gain[:], sub_g.rearrange("(p a) -> p a", a=1)).then_inc(s_par, 16)
                sp.dma_start(lam_in[:], lam_vecs.rearrange("(o a) b -> o a b", o=1).to_broadcast([P, 4, COMP])
                             ).then_inc(s_par, 16)
                sp.dma_start(cpar[:], conv_p.rearrange("(c p) n -> p c n", p=P)).then_inc(s_par, 16)

            def load(m, slot):
                if reused(m):
                    sp.wait_ge(s_xn, m - 1)
                if rows(m) == META:
                    sp.dma_start(x_in[0:META, slot, :], meta).then_inc(s_x[slot], 16)
                else:
                    sp.dma_start(x_in[:, slot, :], x[bass.ds((m - 1) * P, P), :]).then_inc(s_x[slot], 16)
                if isinstance(m, int) and m == 1:
                    sp.dma_start(wv[:], w_in_v[:, :, 2 * AW:3 * AW]).then_inc(s_wv, 16)

            over_tiles(sp, load)

            def weights(first, second, used0=None, used1=None):
                if used0:
                    sp.wait_ge(*used0)
                sp.dma_start(w_slot[:, 0], w_in_v[:, :, first]).then_inc(s_w[0], 16)
                if used1:
                    sp.wait_ge(*used1)
                sp.dma_start(w_slot[:, 1], w_in_v[:, :, second]).then_inc(s_w[1], 16)

            A0, G0 = 3 * AW, 3 * AW + CG * P
            weights(bass.ds(G0, P), bass.ds(A0, P))
            with sp.Fori(1, CG) as c:
                weights(bass.ds(c * P + G0, P), bass.ds(c * P + A0, P), (s_gproj, 3 * c), (s_aproj, 3 * c))
                sp.wait_ge(s_cout, c)
                sp.dma_start(mix_dram[:, :, HEADS - 1 + c, :].rearrange("t p n -> p t n"),
                             conv_out[:].rearrange("p (t n) -> p t n", n=P)).then_inc(s_cst, 16)
            weights(bass.ds(0, P), bass.ds(AW, P), (s_gproj, 3 * CG), (s_aproj, 3 * CG))
            sp.wait_ge(s_cout, CG)
            sp.dma_start(mix_dram[:, :, KC - 1, :].rearrange("t p n -> p t n"),
                         conv_out[:].rearrange("p (t n) -> p t n", n=P)).then_inc(s_cst, 16)
            with sp.Fori(1, HEADS) as h:
                weights(bass.ds(h * P, P), bass.ds(h * P + AW, P), (s_qk, 6 * h - 3), (s_qk, 6 * h))
                sp.wait_ge(s_ho, 2 * h)
                sp.dma_start(mix_dram[:, :, h - 1, :].rearrange("t p n -> p t n"),
                             head_out[:].rearrange("p (t n) -> p t n", n=P)).then_inc(s_hst, 16)
            sp.wait_ge(s_ho, 2 * HEADS)
            sp.dma_start(mix_dram[:, :, HEADS - 1, :].rearrange("t p n -> p t n"),
                         head_out[:].rearrange("p (t n) -> p t n", n=P)).then_inc(s_hst, 16)
            sp.wait_ge(s_cst, 16 * CG)
            sp.wait_ge(s_hst, 16 * HEADS)

        @block.scalar
        def _(act):
            act.wait_ge(s_lam, 2)
            act.activation(lam_s[:, 2:4], lam_s[:, 0:2], ACT.Exp).then_inc(s_lam, 1)

            def values(m, slot):
                act.wait_ge(s_v, m + 1)
                act.sem_inc(s_gate, 1)
                out = v_meta[:] if rows(m) == META else v_all[:, bass.ds(m - 1, 1), :].rearrange("p a n -> p (a n)")
                act.activation(out, banks[4 + slot][0:rows(m), :], ACT.Copy).then_inc(s_vs, 1)

            def norm(m, slot):
                n = rows(m)
                act.wait_ge(s_x[slot], 8 * (m + slot + 1))
                if reused(m):
                    act.wait_ge(s_xT, m - 1)
                act.activation(xn[0:n, slot, :], x_in[0:n, slot, :], ACT.Square,
                               accum_out=ssum[0:n, slot:slot + 1]).then_inc(s_ss, 1)
                act.wait_ge(s_var, m + 1)
                act.activation(ssum[0:n, slot:slot + 1], rstd[0:n, slot:slot + 1], ACT.Sqrt).then_inc(s_std, 1)
                act.wait_ge(s_rstd, m + 1)
                act.activation(xn[0:n, slot, :], x_in[0:n, slot, :], ACT.Copy,
                               scale=rstd[0:n, slot:slot + 1]).then_inc(s_xn, 1)
                if not (isinstance(m, int) and m == 0):
                    values(m - 1, 1 - slot)

            over_tiles(act, norm)
            values(NM - 1, 1)

            def sigmoids(c):
                for n, (lo, w) in enumerate(SEGS):
                    act.wait_ge(s_gproj, 3 * c + n + 1)
                    if not isinstance(c, int):
                        act.wait_ge(s_u, 3 * c)
                    act.activation(gate_sig[:, lo:lo + w], banks[n][:, 0:w], ACT.Sigmoid).then_inc(s_sig, 1)

            def conv_norm(c):
                act.wait_ge(s_yc, 2 * (c + 1))
                act.activation(ysq[:], yc[:], ACT.Square).then_inc(s_ysq, 1)
                act.wait_ge(s_yvar, c + 1)
                act.wait_ge(s_const, 4)
                for b in range(2):
                    act.activation(ystd[:, b * 512:b * 512 + 512], banks[6 + b][:], ACT.Sqrt,
                                   bias=eps_col[:]).then_inc(s_ystd, 1)
                act.wait_ge(s_yn, c + 1)
                act.sem_inc(s_gate, 1)
                cp = cpar[:, bass.ds(c, 1), :].rearrange("p a n -> p (a n)")
                act.activation(conv_out[:], yc[:], ACT.Silu, scale=cp[:, TAPS + 1:TAPS + 2],
                               bias=cp[:, TAPS + 2:TAPS + 3]).then_inc(s_cout, 1)

            def projected(h, piece):
                n = piece % 3
                lo, w = SEGS[n]
                act.wait_ge(s_qk, 6 * h + piece + 1)
                dst = q_next if piece < 3 else k_next
                act.activation(dst[:, lo:lo + w], banks[n][:, 0:w], ACT.Copy).then_inc(s_qks, 1)

            sigmoids(0)
            with act.Fori(0, CG - 1) as c:
                act.wait_ge(s_par, 64)
                sigmoids(c + 1)
                conv_norm(c)
                act.wait_ge(s_cst, 16 * (c + 1))
            for piece in range(6):
                projected(0, piece)
            conv_norm(CG - 1)

            def outputs(h, i):
                act.wait_ge(s_mt, NT * h + i + 1)
                act.activation(aT_meta[:], banks[7][0:META, 0:P], ACT.Copy).then_inc(s_mts, 1)
                for g in range(GROUPS[i]):
                    e = gr_before(i) + g
                    nb = min(4, i + 1 - 4 * g)
                    act.wait_ge(s_at, GR_H * h + e + 1)
                    act.activation(aT[:, e % 2, 0:nb * P], banks[5 + e % 2][:, 0:nb * P], ACT.Copy).then_inc(s_ats, 1)
                act.wait_ge(s_pv, NT * h + i + 1)
                if i == 0:
                    act.wait_ge(s_oT, h + 1)
                act.activation(o_all[:, i, :], banks[7][:, P:2 * P], ACT.Copy).then_inc(s_o, 1)

            def head(h, last):
                for i in range(NT):
                    nk = META + P * (i + 1)
                    act.wait_ge(s_nm, 2 * (NT * h + i + 1))
                    for c in range(2):
                        act.activation(z[:, i % 2, c, 0:nk], z[:, i % 2, c, 0:nk], ACT.Exp, scale=SCALE,
                                       bias=nmax[:, i % 2, c:c + 1],
                                       accum_out=zsum[:, i % 2, c:c + 1]).then_inc(s_exp, 1)
                    if not last and 1 <= i <= 4:
                        projected(h + 1, i - 1)
                    if i >= 1:
                        outputs(h, i - 1)
                outputs(h, NT - 1)
                if not last:
                    projected(h + 1, 4)
                    projected(h + 1, 5)
                act.wait_ge(s_fin, 4 * h + 3)
                act.activation(o_rs[:], o_ss[:], ACT.Sqrt).then_inc(s_ostd, 1)

            with act.Fori(0, HEADS - 1) as h:
                head(h, False)
            head(HEADS - 1, True)

        @block.vector
        def _(dve):
            dve.wait_ge(s_par, 64)
            for n in range(2):
                dve.tensor_tensor_reduce(lam_in[:, 2 * n, :], lam_in[:, 2 * n, :], lam_in[:, 2 * n + 1, :], 1.0, 0.0,
                                         ALU.mult, ALU.add, lam_s[:, n:n + 1]).then_inc(s_lam, 1)
            dve.wait_ge(s_lam, 3)
            dve.tensor_tensor(lam_s[:, 0:1], lam_s[:, 2:3], lam_s[:, 3:4], ALU.subtract).then_inc(s_lam, 1)
            dve.wait_ge(s_lam, 4)
            dve.tensor_scalar(lam_s[:, 1:2], lam_s[:, 0:1], LAM_INIT, None, ALU.add).then_inc(s_lam, 1)
            dve.tensor_scalar(sub_gain[:], sub_gain[:], 1.0 - LAM_INIT, None, ALU.mult).then_inc(s_lam, 1)
            lam = lam_s[:, 1:2]
            dve.wait_ge(s_const, 10)
            dve.tensor_scalar(bias[:], bias[:], SLOPE0 / SCALE, None, ALU.mult).then_inc(s_bias, 1)

            def tile(m, slot):
                n = rows(m)
                dve.wait_ge(s_ss, m + 1)
                dve.tensor_scalar(rstd[0:n, slot:slot + 1], ssum[0:n, slot:slot + 1], 1.0 / D, EPS, ALU.mult,
                                  ALU.add).then_inc(s_var, 1)
                dve.wait_ge(s_std, m + 1)
                dve.reciprocal(rstd[0:n, slot:slot + 1], ssum[0:n, slot:slot + 1]).then_inc(s_rstd, 1)
                dve.wait_ge(s_xT, m + 1)
                if reused(m):
                    dve.wait_ge(s_v, m - 1)
                    dve.wait_ge(s_xTall, m - 1)
                for b in range(2):
                    ins = dve.tensor_tensor(
                        xnT_tile[:, slot, 4 * b:4 * b + 4, 0:n],
                        x_banks[slot][b][:, 0:4 * P].rearrange("p (k n) -> p k n", n=P)[:, :, 0:n],
                        g1_cols[:, 4 * b:4 * b + 4].unsqueeze(2).to_broadcast([P, 4, n]), ALU.mult)
                ins.then_inc(s_xTs, 1)

            over_tiles(dve, tile)

            def gated(c):
                if not isinstance(c, int):
                    dve.wait_ge(s_tap, TAPS * c)
                for n, (lo, w) in enumerate(SEGS):
                    dve.wait_ge(s_aproj, 3 * c + n + 1)
                    dve.wait_ge(s_sig, 3 * c + n + 1)
                    dve.tensor_tensor(u_pad[:, TAPS - 1 + lo:TAPS - 1 + lo + w], banks[3 + n][:, 0:w],
                                      gate_sig[:, lo:lo + w], ALU.mult).then_inc(s_u, 1)

            def conv(c):
                cp = cpar[:, bass.ds(c, 1), :].rearrange("p a n -> p (a n)")
                dve.wait_ge(s_u, 3 * c + 3)
                dve.tensor_scalar(y[:], u_pad[:, META:META + SEQ], cp[:, 0:1], cp[:, TAPS:TAPS + 1], ALU.mult,
                                  ALU.add).then_inc(s_tap, 1)
                for k in range(1, TAPS):
                    dve.wait_ge(s_tap, TAPS * c + k)
                    dve.scalar_tensor_tensor(out=y[:], in0=u_pad[:, META + k:META + k + SEQ], scalar=cp[:, k:k + 1],
                                             in1=y[:], op0=ALU.mult, op1=ALU.add).then_inc(s_tap, 1)
                dve.wait_ge(s_mean, c + 1)
                for b in range(2):
                    half = slice(b * 512, b * 512 + 512)
                    dve.tensor_tensor(yc[:, half], y[:, half], banks[6 + b][:], ALU.subtract).then_inc(s_yc, 1)

            def conv_scaled(c):
                dve.wait_ge(s_ystd, 2 * (c + 1))
                dve.reciprocal(ystd[:], ystd[:]).then_inc(s_yrec, 1)
                dve.wait_ge(s_yrec, c + 1)
                dve.tensor_tensor(yc[:], yc[:], ystd[:], ALU.mult).then_inc(s_yn, 1)

            gated(0)
            with dve.Fori(0, CG - 1) as c:
                conv(c)
                gated(c + 1)
                conv_scaled(c)
                dve.wait_ge(s_cout, c + 1)
            conv(CG - 1)
            conv_scaled(CG - 1)

            def weights(h, i):
                nk = META + P * (i + 1)
                dve.wait_ge(s_exp, 2 * (NT * h + i + 1))
                dve.reciprocal(zinv[:, i % 2, :], zsum[:, i % 2, :]).then_inc(s_inv, 1)
                dve.wait_ge(s_inv, 2 * (NT * h + i) + 1)
                dve.tensor_tensor(zinv[:, i % 2, 1:2], zinv[:, i % 2, 1:2], lam, ALU.mult).then_inc(s_inv, 1)
                dve.wait_ge(s_t1, NT * h + i + 1)
                dve.scalar_tensor_tensor(out=z[:, i % 2, 0, 0:nk], in0=z[:, i % 2, 0, 0:nk],
                                         scalar=zinv[:, i % 2, 0:1], in1=z[:, i % 2, 1, 0:nk], op0=ALU.mult,
                                         op1=ALU.subtract).then_inc(s_a, 1)

            def head(h, last):
                dve.wait_ge(s_bias, h + 1)
                for i in range(NT):
                    off = (NT - 1 - i) * P
                    if i >= 2:
                        dve.wait_ge(s_at, GR_H * h + gr_before(i - 1))
                        dve.wait_ge(s_mt, NT * h + i - 1)
                    for c in range(2):
                        for n in range(CHUNKS[i]):
                            e = sc_before(i, c) + n
                            lo, hi = chunk(i, n)
                            dve.wait_ge(s_sc, SC_H * h + e + 1)
                            dve.sem_inc(s_gate, 1)
                            dve.tensor_tensor_reduce(z[:, i % 2, c, lo:hi], banks[3 + e % 2][:, 0:hi - lo],
                                                     bias[:, off + lo:off + hi], 1.0, NEG, ALU.add, ALU.max,
                                                     zmax[:, i % 2, c, n:n + 1]).then_inc(s_z, 1)
                    dve.wait_ge(s_z, SC_H * h + sc_before(i + 1, 0) if i + 1 < NT else SC_H * (h + 1))
                    dve.tensor_reduce(nmax[:, i % 2, :], zmax[:, i % 2, :, 0:CHUNKS[i]], AX.X,
                                      ALU.max).then_inc(s_nm, 1)
                    dve.wait_ge(s_nm, 2 * (NT * h + i) + 1)
                    dve.tensor_scalar(nmax[:, i % 2, :], nmax[:, i % 2, :], -SCALE, None, ALU.mult).then_inc(s_nm, 1)
                    if i >= 1:
                        weights(h, i - 1)
                weights(h, NT - 1)
                if not last:
                    dve.tensor_scalar(bias[:], bias[:], SLOPE0, None, ALU.mult).then_inc(s_bias, 1)
                dve.wait_ge(s_o, NT * (h + 1))
                dve.tensor_tensor(o_sq[:], o_all[:], o_all[:], ALU.mult).then_inc(s_fin, 1)
                dve.wait_ge(s_fin, 4 * h + 1)
                dve.tensor_reduce(o_ss[:], o_sq[:], AX.X, ALU.add).then_inc(s_fin, 1)
                dve.wait_ge(s_fin, 4 * h + 2)
                dve.tensor_scalar(o_ss[:], o_ss[:], 1.0 / P, EPS, ALU.mult, ALU.add).then_inc(s_fin, 1)
                dve.wait_ge(s_ostd, 2 * h + 1)
                dve.reciprocal(o_rs[:], o_rs[:]).then_inc(s_ostd, 1)
                dve.wait_ge(s_ostd, 2 * h + 2)
                dve.tensor_tensor(o_all[:], o_all[:], o_rs[:].unsqueeze(2).to_broadcast([P, NT, P]),
                                  ALU.mult).then_inc(s_fin, 1)
                dve.wait_ge(s_oT, h + 2)
                for b in range(2):
                    dve.tensor_scalar(head_out[:, b * 512:b * 512 + 512], banks[3 + b][:], sub_gain[:], None,
                                      ALU.mult).then_inc(s_ho, 1)
                if not last:
                    dve.wait_ge(s_hst, 16 * (h + 1))

            with dve.Fori(0, HEADS - 1) as h:
                head(h, False)
            head(HEADS - 1, True)

        @block.tensor
        def _(pe):
            pe.wait_ge(s_const, 10)
            pe.sem_inc(s_oT, 1)

            def tile(m, slot):
                n = rows(m)
                pe.wait_ge(s_xn, m + 1)
                if reused(m):
                    pe.wait_ge(s_xTs, m - 1)
                for k in range(KC):
                    ins = pe.transpose(x_banks[slot][k // 4][:, (k % 4) * P:(k % 4) * P + n],
                                       xn[0:n, slot, k * P:(k + 1) * P], ident[0:n, 0:n])
                ins.then_inc(s_xT, 1)
                if isinstance(m, int) and m == 0:
                    pe.wait_ge(s_wv, 16)
                pe.wait_ge(s_xTs, m + 1)
                if reused(m):
                    pe.wait_ge(s_vs, m - 1)
                for k in range(KC):
                    ins = pe.matmul(banks[4 + slot][0:n, :], xnT_tile[:, slot, k, 0:n], wv[:, k, :],
                                    start=(k == 0), stop=(k == KC - 1))
                ins.then_inc(s_v, 1)

            over_tiles(pe, tile)
            pe.wait_ge(s_xTs, NM)
            pe.wait_ge(s_vs, NM)
            pe.wait_ge(s_xTall, NM)

            def project(slot, seg, bank):
                lo, w = SEGS[seg]
                for k in range(KC):
                    ins = pe.matmul(bank[:, 0:w], w_slot[:, slot, k, :], xnT[:, k, lo:lo + w],
                                    start=(k == 0), stop=(k == KC - 1))
                return ins

            def project_conv(c):
                for slot, done, free, at in ((0, s_gproj, s_sig, 0), (1, s_aproj, s_u, 3)):
                    pe.wait_ge(s_w[slot], 16 * (c + 1))
                    for n in range(3):
                        if not isinstance(c, int):
                            pe.wait_ge(free, 3 * (c - 1) + n + 1)
                        project(slot, n, banks[at + n]).then_inc(done, 1)

            def group_norm(c):
                pe.wait_ge(s_tap, TAPS * (c + 1))
                for b in range(2):
                    ins = pe.matmul(banks[6 + b][:], group_mean[:], y[:, b * 512:b * 512 + 512], start=True, stop=True)
                ins.then_inc(s_mean, 1)
                pe.wait_ge(s_ysq, c + 1)
                for b in range(2):
                    ins = pe.matmul(banks[6 + b][:], group_mean[:], ysq[:, b * 512:b * 512 + 512],
                                    start=True, stop=True)
                ins.then_inc(s_yvar, 1)

            def project_head(h, piece):
                slot, n = piece // 3, piece % 3
                if n == 0:
                    pe.wait_ge(s_w[slot], 16 * (CG + h + 1))
                if isinstance(h, int) and h == 0 and piece < 3:
                    pe.wait_ge(s_sig, 3 * CG)
                else:
                    pe.wait_ge(s_qks, 6 * h + piece - 2)
                project(slot, n, banks[n]).then_inc(s_qk, 1)

            project_conv(0)
            with pe.Fori(0, CG - 1) as c:
                project_conv(c + 1)
                group_norm(c)
            for piece in range(6):
                project_head(0, piece)
            group_norm(CG - 1)
            pe.wait_ge(s_u, 3 * CG)
            pe.wait_ge(s_ystd, 2 * CG)

            def scores(h, i):
                for c in range(2):
                    for n in range(CHUNKS[i]):
                        e = sc_before(i, c) + n
                        lo, hi = chunk(i, n)
                        if e >= 2:
                            pe.wait_ge(s_z, SC_H * h + e - 1)
                        pe.matmul(banks[3 + e % 2][:, 0:hi - lo], qT[c * COMP:(c + 1) * COMP, i * P:(i + 1) * P],
                                  kT[c * COMP:(c + 1) * COMP, lo:hi], start=True, stop=True).then_inc(s_sc, 1)

            def output(h, i):
                pe.wait_ge(s_a, NT * h + i + 1)
                if i >= 1:
                    pe.wait_ge(s_o, NT * h + i)
                elif isinstance(h, int):
                    pe.wait_ge(s_o, NT * h)
                pe.transpose(banks[7][0:META, 0:P], z[:, i % 2, 0, 0:META], ident[:]).then_inc(s_mt, 1)
                for g in range(GROUPS[i]):
                    e = gr_before(i) + g
                    if e >= 2:
                        pe.wait_ge(s_ats, GR_H * h + e - 1)
                    for b in range(4 * g, min(4 * g + 4, i + 1)):
                        ins = pe.transpose(banks[5 + e % 2][:, (b % 4) * P:(b % 4 + 1) * P],
                                           z[:, i % 2, 0, META + b * P:META + (b + 1) * P], ident[:])
                    ins.then_inc(s_at, 1)
                cols = bass.ds(h * P, P)
                pe.wait_ge(s_mts, NT * h + i + 1)
                pe.sem_inc(s_gate, 1)
                pe.matmul(banks[7][:, P:2 * P], aT_meta[:], v_meta[:, cols], start=True, stop=False)
                for g in range(GROUPS[i]):
                    e = gr_before(i) + g
                    pe.wait_ge(s_ats, GR_H * h + e + 1)
                    for b in range(4 * g, min(4 * g + 4, i + 1)):
                        ins = pe.matmul(banks[7][:, P:2 * P], aT[:, e % 2, (b % 4) * P:(b % 4 + 1) * P],
                                        v_all[:, b, cols], start=False, stop=(b == i))
                ins.then_inc(s_pv, 1)

            def head(h, last):
                pe.wait_ge(s_cur, 2 * (h + 1))
                for i in range(NT):
                    scores(h, i)
                    if not last and 1 <= i <= 4:
                        project_head(h + 1, i - 1)
                    if i >= 1:
                        output(h, i - 1)
                output(h, NT - 1)
                if not last:
                    project_head(h + 1, 4)
                    project_head(h + 1, 5)
                pe.wait_ge(s_fin, 4 * (h + 1))
                for t in range(NT):
                    ins = pe.transpose(banks[3 + t // 4][:, (t % 4) * P:(t % 4 + 1) * P], o_all[:, t, :], ident[:])
                ins.then_inc(s_oT, 1)

            with pe.Fori(0, HEADS - 1) as h:
                head(h, False)
            head(HEADS - 1, True)


ROUTE_STEPS = 12
PREP_STEPS = 4
LAST_STEPS = 3


def expert_phase(nc, x, mix_dram, w_out, g2, wq, subkeys_t, table, g_final, out):
    ctx = ExitStack()
    with ctx:
        def sb(name, shape, dt=F32):
            return ctx.enter_context(nc.sbuf_tensor(name, shape, dt))

        def pb(name, shape):
            return ctx.enter_context(nc.psum_tensor(name, shape, F32))

        def sem(name):
            return ctx.enter_context(nc.semaphore(name))

        ident = sb("identB", [P, P])
        iota_i = sb("iota_i", [P, TOPK], I32)
        iota_f = sb("iota_f", [P, TOPK])
        w_out_s = sb("w_out_s", [P, KC, D])
        wq_s = sb("wq_s", [P, KC, PH * 2 * QH])
        keys_s = sb("keys_s", [P, PH * 2, KEYS])
        g2_row = sb("g2_row", [P, D])
        gf_row = sb("gf_row", [P, D])
        ring = sb("ring", [P, RING, 2 * D])
        mix_t = sb("mix_t", [P, KC, P])
        h_next = sb("h_next", [P, D])
        xn_next = sb("xn_next", [P, D])
        xn_cur = sb("xn_cur", [P, D])
        xnT_cur = sb("xnT_cur", [P, KC, P])
        nrm = sb("nrm", [P, 4])
        q_s = sb("q_s", [P, 2 * QH])
        qT_s = sb("qT_s", [P, 2, P])
        top_v = sb("top_v", [P, 2, TOPK])
        top_i = sb("top_i", [P, 2, TOPK], U32)
        cand = sb("cand", [P, CAND])
        cand_t = sb("cand_t", [P, CAND])
        c_top = sb("c_top", [P, TOPK])
        c_idx = sb("c_idx", [P, TOPK], U32)
        c_ab = sb("c_ab", [P, 2, TOPK], U32)
        hot = sb("hot", [P, 2 * TOPK, TOPK])
        pick = sb("pick", [P, 2, TOPK])
        neg_top = sb("neg_top", [P, 1])
        g_exp = sb("g_exp", [P, TOPK])
        g_sum = sb("g_sum", [P, 2])
        e_next = sb("e_next", [P, TOPK], U32)
        gate_next = sb("gate_next", [P, TOPK])
        e_cur = sb("e_cur", [P, TOPK], U32)
        gate_cur = sb("gate_cur", [P, TOPK])
        dots = sb("dots", [P, TOPK])
        gelu = sb("gelu", [P, TOPK])
        diag = sb("diag", [P, DIAGS, P])

        acc = pb("acc", [P, D])
        proj = pb("projB", [P, D])
        q_ps = pb("q_ps", [P, 512])
        qT_ps = pb("qT_ps", [P, 512])
        s_ps = pb("s_ps", [P, 512])

        b_const = sem("b_const")
        b_gate = sem("b_gate")
        b_par = sem("b_par")
        b_wout = sem("b_wout")
        b_wq = [sem("b_wq0"), sem("b_wq1")]
        b_mix = sem("b_mix")
        b_h = sem("b_h")
        b_op = sem("b_op")
        b_hsum = sem("b_hsum")
        b_prep = sem("b_prep")
        b_pss = sem("b_pss")
        b_pstd = sem("b_pstd")
        b_xT = sem("b_xT")
        b_xTs = sem("b_xTs")
        b_q = sem("b_q")
        b_qs = sem("b_qs")
        b_qT = sem("b_qT")
        b_qTs = sem("b_qTs")
        b_s = sem("b_s")
        b_r = sem("b_r")
        b_gexp = sem("b_gexp")
        b_route = sem("b_route")
        b_gates = sem("b_gates")
        b_e = sem("b_e")
        b_row = [sem(f"b_row{r}") for r in range(RING)]
        b_free = sem("b_free")
        b_dot = sem("b_dot")
        b_gelu = sem("b_gelu")
        b_gcur = sem("b_gcur")
        b_diag = sem("b_diag")
        b_lss = sem("b_lss")
        b_lstd = sem("b_lstd")
        b_last = sem("b_last")
        b_out = sem("b_out")

        block = ctx.enter_context(nc.Block())
        w_out_v = w_out.rearrange("(k p) n -> p k n", p=P)
        wq_v = wq.rearrange("(k p) n -> p k n", p=P)
        HALF = [slice(0, 512), slice(512, 1024)]

        def over_heads(eng, t, step):
            step(t * PH, "first")
            with eng.Fori(1, PH - 1) as h:
                step(t * PH + h, "middle")
            step(t * PH + (PH - 1), "last")

        @block.gpsimd
        def _(pool):
            pool.memset(ident[:], 0.0).then_inc(b_const, 1)
            pool.iota(iota_i[:], [[1, TOPK]], base=0, channel_multiplier=0).then_inc(b_const, 1)
            pool.wait_ge(b_const, 2)
            pool.affine_select(out=ident[:], in_=ident[:], compare_op=ALU.not_equal, fill=1.0, base=0,
                               pattern=[[-1, P]], channel_multiplier=1).then_inc(b_const, 1)
            pool.tensor_copy(iota_f[:], iota_i[:]).then_inc(b_const, 1)

            def step(n, kind):
                pool.wait_ge(b_route, n + 1)
                pool.sem_inc(b_gate, 1)
                for k in range(TOPK):
                    pool.wait_ge(b_free, TOPK * n + k + 1)
                    pool.sem_inc(b_gate, 1)
                    if k % RING == 0:
                        cols = slice(k, k + RING)
                        pool.tensor_copy(e_cur[:, cols], e_next[:, cols]).then_inc(b_e, 1)
                        pool.wait_ge(b_e, TOPK // RING * n + k // RING + 1)
                        pool.sem_inc(b_gate, 1)
                    pool.indirect_dma_start(out=ring[:, k % RING, :], out_offset=None, in_=table[:, :],
                                            in_offset=bass.IndirectOffsetOnAxis(ap=e_cur[:, k:k + 1], axis=0)
                                            ).then_inc(b_row[k % RING], 16)

            with pool.Fori(0, NT) as t:
                over_heads(pool, t, step)

        @block.sync
        def _(sp):
            sp.dma_start(mix_t[:], mix_dram[0, :, :, :]).then_inc(b_mix, 16)
            sp.dma_start(h_next[:], x[0:P, :]).then_inc(b_h, 16)
            sp.dma_start(w_out_s[:], w_out_v).then_inc(b_wout, 16)
            sp.dma_start(g2_row[:], g2.rearrange("(a n) -> a n", a=1).to_broadcast([P, D])).then_inc(b_par, 16)
            sp.dma_start(keys_s[:], subkeys_t).then_inc(b_par, 16)
            sp.dma_start(wq_s[:, :, 0:2 * QH], wq_v[:, :, 0:2 * QH]).then_inc(b_wq[0], 16)
            sp.dma_start(gf_row[:], g_final.rearrange("(a n) -> a n", a=1).to_broadcast([P, D])).then_inc(b_par, 16)
            sp.dma_start(wq_s[:, :, 2 * QH:], wq_v[:, :, 2 * QH:]).then_inc(b_wq[1], 16)
            sp.sem_inc(b_out, 16)
            with sp.Fori(0, NT) as t:
                nxt = (t + 1) % NT
                sp.wait_ge(b_op, t + 1)
                sp.dma_start(mix_t[:], mix_dram[bass.ds(nxt, 1), :, :, :].rearrange("a p k n -> p (a k) n")
                             ).then_inc(b_mix, 16)
                sp.wait_ge(b_free, PH * TOPK * t + RING + 1)
                sp.dma_start(h_next[:], x[bass.ds(nxt * P, P), :]).then_inc(b_h, 16)
                sp.wait_ge(b_last, LAST_STEPS * (t + 1))
                sp.dma_start(out[bass.ds(t * P, P), :], xn_next[:]).then_inc(b_out, 16)
            sp.wait_ge(b_out, 16 * (NT + 1))
            sp.wait_ge(b_mix, 16 * (NT + 1))
            sp.wait_ge(b_h, 16 * (NT + 1))

        @block.scalar
        def _(act):
            def square_and_root(p):
                act.wait_ge(b_hsum, p + 1)
                if not isinstance(p, int):
                    act.wait_ge(b_out, 16 * p)
                act.activation(xn_next[:], h_next[:], ACT.Square, accum_out=nrm[:, 0:1]).then_inc(b_pss, 1)
                act.wait_ge(b_prep, PREP_STEPS * p + 1)
                act.activation(nrm[:, 0:1], nrm[:, 1:2], ACT.Sqrt).then_inc(b_pstd, 1)

            def transposed(p):
                act.wait_ge(b_xT, p + 1)
                act.activation(xnT_cur[:].rearrange("p k n -> p (k n)"), proj[:], ACT.Copy).then_inc(b_xTs, 1)

            def queries(r):
                act.wait_ge(b_q, r + 1)
                act.activation(q_s[:], q_ps[:, 0:2 * QH], ACT.Copy).then_inc(b_qs, 1)

            def queries_t(r):
                act.wait_ge(b_qT, r + 1)
                act.activation(qT_s[:].rearrange("p a n -> p (a n)"), qT_ps[:, 0:2 * P], ACT.Copy).then_inc(b_qTs, 1)

            def gate_exp(r):
                act.wait_ge(b_r, ROUTE_STEPS * r + 10)
                act.activation(g_exp[:], c_top[:], ACT.Exp, bias=neg_top[:], accum_out=g_sum[:, 0:1]).then_inc(b_gexp, 1)

            def step(n, kind):
                if kind == "last":
                    transposed((n + 1) // PH if isinstance(n, int) else t_var[0] + 1)
                for k in range(TOPK):
                    if k == 1:
                        queries(n + 1)
                    if k == 3:
                        queries_t(n + 1)
                    if k == 9:
                        gate_exp(n + 1)
                    act.wait_ge(b_dot, TOPK * n + k + 1)
                    if k == 0:
                        act.wait_ge(b_gcur, n + 1)
                    act.activation(gelu[:, k:k + 1], dots[:, k:k + 1], ACT.Gelu).then_inc(b_gelu, 1)
                if kind == "first":
                    square_and_root(t_var[0] + 1)

            t_var = [0]
            square_and_root(0)
            transposed(0)
            queries(0)
            queries_t(0)
            gate_exp(0)
            with act.Fori(0, NT) as t:
                t_var[0] = t
                over_heads(act, t, step)
                act.wait_ge(b_free, PH * TOPK * (t + 1) + RING)
                act.wait_ge(b_prep, PREP_STEPS * (t + 2))
                act.activation(xn_next[:], acc[:], ACT.Square, accum_out=nrm[:, 2:3]).then_inc(b_lss, 1)
                act.wait_ge(b_last, LAST_STEPS * t + 1)
                act.activation(nrm[:, 2:3], nrm[:, 3:4], ACT.Sqrt).then_inc(b_lstd, 1)

        @block.vector
        def _(dve):
            dve.wait_ge(b_const, 4)
            dve.wait_ge(b_par, 48)

            def residual(p):
                dve.wait_ge(b_h, 16 * (p + 1))
                dve.wait_ge(b_op, p + 1)
                dve.tensor_tensor(h_next[:], h_next[:], proj[:], ALU.add).then_inc(b_hsum, 1)

            def normalise(p):
                dve.wait_ge(b_pss, p + 1)
                dve.tensor_scalar(nrm[:, 1:2], nrm[:, 0:1], 1.0 / D, EPS, ALU.mult, ALU.add).then_inc(b_prep, 1)
                dve.wait_ge(b_pstd, p + 1)
                dve.reciprocal(nrm[:, 1:2], nrm[:, 0:1]).then_inc(b_prep, 1)
                dve.wait_ge(b_prep, PREP_STEPS * p + 2)
                dve.scalar_tensor_tensor(out=xn_next[:], in0=h_next[:], scalar=nrm[:, 1:2], in1=g2_row[:],
                                         op0=ALU.mult, op1=ALU.mult).then_inc(b_prep, 1)

            def become_current(p):
                dve.wait_ge(b_prep, PREP_STEPS * p + 3)
                dve.wait_ge(b_xT, p + 1)
                dve.tensor_copy(xn_cur[:], xn_next[:]).then_inc(b_prep, 1)

            def after(value):
                dve.wait_ge(b_r, value)
                dve.sem_inc(b_gate, 1)

            def route(r):
                s0 = ROUTE_STEPS * r
                half = [s_ps[:, p * KEYS:(p + 1) * KEYS] for p in range(2)]
                rest = [cand_t[:, p * KEYS:(p + 1) * KEYS] for p in range(2)]
                lo, hi = slice(0, 8), slice(8, TOPK)
                dve.wait_ge(b_s, r + 1)
                dve.sem_inc(b_gate, 1)
                for p in range(2):
                    ins = dve.max(top_v[:, p, lo], half[p])
                ins.then_inc(b_r, 1)
                after(s0 + 1)
                for p in range(2):
                    dve.max_index(top_i[:, p, lo], top_v[:, p, lo], half[p])
                    ins = dve.match_replace(rest[p], top_v[:, p, lo], half[p], NEG)
                ins.then_inc(b_r, 1)
                after(s0 + 2)
                for p in range(2):
                    ins = dve.max(top_v[:, p, hi], rest[p])
                ins.then_inc(b_r, 1)
                after(s0 + 3)
                for p in range(2):
                    dve.max_index(top_i[:, p, hi], top_v[:, p, hi], rest[p])
                dve.tensor_tensor(cand[:].rearrange("p (a b) -> p a b", b=TOPK),
                                  top_v[:, 0, :].unsqueeze(2).to_broadcast([P, TOPK, TOPK]),
                                  top_v[:, 1, :].unsqueeze(1).to_broadcast([P, TOPK, TOPK]), ALU.add).then_inc(b_r, 1)
                after(s0 + 4)
                dve.max(c_top[:, lo], cand[:]).then_inc(b_r, 1)
                after(s0 + 5)
                dve.max_index(c_idx[:, lo], c_top[:, lo], cand[:])
                dve.tensor_scalar(neg_top[:], c_top[:, 0:1], -1.0, None, ALU.mult)
                dve.match_replace(cand_t[:], c_top[:, lo], cand[:], NEG).then_inc(b_r, 1)
                after(s0 + 6)
                dve.max(c_top[:, hi], cand_t[:]).then_inc(b_r, 1)
                after(s0 + 7)
                dve.max_index(c_idx[:, hi], c_top[:, hi], cand_t[:]).then_inc(b_r, 1)
                dve.wait_ge(b_r, s0 + 8)
                dve.tensor_scalar(c_ab[:, 0, :], c_idx[:], 4, None, ALU.logical_shift_right)
                dve.tensor_scalar(c_ab[:, 1, :], c_idx[:], TOPK - 1, None, ALU.bitwise_and).then_inc(b_r, 1)
                dve.wait_ge(b_r, s0 + 9)
                dve.tensor_tensor(hot[:], c_ab[:].rearrange("p a k -> p (a k)").unsqueeze(2).to_broadcast([P, 2 * TOPK, TOPK]),
                                  iota_f[:].unsqueeze(1).to_broadcast([P, 2 * TOPK, TOPK]),
                                  ALU.is_equal).then_inc(b_r, 1)
                dve.wait_ge(b_r, s0 + 10)
                hot4 = hot[:].rearrange("p (a k) j -> p a k j", a=2)
                dve.tensor_tensor(hot4, hot4, top_i[:].unsqueeze(2).to_broadcast([P, 2, TOPK, TOPK]),
                                  ALU.mult).then_inc(b_r, 1)
                dve.wait_ge(b_r, s0 + 11)
                dve.tensor_reduce(pick[:].rearrange("p a k -> p (a k)"), hot[:], AX.X, ALU.add).then_inc(b_r, 1)

            def experts(r):
                dve.wait_ge(b_r, ROUTE_STEPS * (r + 1))
                if not (isinstance(r, int) and r == 0):
                    dve.wait_ge(b_e, TOPK // RING * r)
                dve.scalar_tensor_tensor(out=e_next[:], in0=pick[:, 0, :], scalar=float(KEYS), in1=pick[:, 1, :],
                                         op0=ALU.mult, op1=ALU.add).then_inc(b_route, 1)

            def gates(r):
                dve.wait_ge(b_gexp, r + 1)
                dve.reciprocal(g_sum[:, 1:2], g_sum[:, 0:1]).then_inc(b_gates, 1)
                dve.wait_ge(b_gates, 2 * r + 1)
                dve.tensor_scalar(gate_next[:], g_exp[:], g_sum[:, 1:2], None, ALU.mult).then_inc(b_gates, 1)

            def diagonal(n, k):
                dve.wait_ge(b_gelu, TOPK * n + k + 1)
                dve.wait_ge(b_free, TOPK * n + k + 1 + RING - DIAGS)
                dve.tensor_scalar(diag[:, k % DIAGS, :], ident[:], gelu[:, k:k + 1], gate_cur[:, k:k + 1], ALU.mult,
                                  ALU.mult).then_inc(b_diag, 1)

            def step(n, kind):
                dve.wait_ge(b_gates, 2 * n + 2)
                dve.tensor_copy(gate_cur[:], gate_next[:]).then_inc(b_gcur, 1)
                for k in range(TOPK):
                    dve.wait_ge(b_row[k % RING], 16 * (TOPK // RING * n + k // RING + 1))
                    dve.tensor_tensor_reduce(ring[:, k % RING, 0:D], ring[:, k % RING, 0:D], xn_cur[:], 1.0, 0.0,
                                             ALU.mult, ALU.add, dots[:, k:k + 1]).then_inc(b_dot, 1)
                    if k >= 1:
                        diagonal(n, k - 1)
                    if k == 6:
                        route(n + 1)
                    if k == 11:
                        gates(n + 1)
                    if k == TOPK - RING:
                        experts(n + 1)
                diagonal(n, TOPK - 1)
                dve.wait_ge(b_diag, TOPK * (n + 1))
                dve.sem_inc(b_gate, 1)
                if kind == "first":
                    residual(t_var[0] + 1)
                    normalise(t_var[0] + 1)

            t_var = [0]
            residual(0)
            normalise(0)
            route(0)
            experts(0)
            gates(0)
            become_current(0)
            with dve.Fori(0, NT) as t:
                t_var[0] = t
                dve.wait_ge(b_prep, PREP_STEPS * (t + 1))
                over_heads(dve, t, step)
                become_current(t + 1)
                dve.wait_ge(b_lss, t + 1)
                dve.tensor_scalar(nrm[:, 3:4], nrm[:, 2:3], 1.0 / D, EPS, ALU.mult, ALU.add).then_inc(b_last, 1)
                dve.wait_ge(b_lstd, t + 1)
                dve.reciprocal(nrm[:, 3:4], nrm[:, 2:3]).then_inc(b_last, 1)
                dve.wait_ge(b_last, LAST_STEPS * t + 2)
                dve.scalar_tensor_tensor(out=xn_next[:], in0=acc[:], scalar=nrm[:, 3:4], in1=gf_row[:],
                                         op0=ALU.mult, op1=ALU.mult).then_inc(b_last, 1)

        @block.tensor
        def _(pe):
            pe.wait_ge(b_const, 3)
            pe.wait_ge(b_wout, 16)
            pe.sem_inc(b_free, RING)

            def project(p, k):
                if k == 0:
                    pe.wait_ge(b_mix, 16 * (p + 1))
                for b in range(2):
                    ins = pe.matmul(proj[:, HALF[b]], mix_t[:, k, :], w_out_s[:, k, HALF[b]],
                                    start=(k == 0), stop=(k == KC - 1))
                if k == KC - 1:
                    ins.then_inc(b_op, 1)

            def transpose_tile(p):
                pe.wait_ge(b_prep, PREP_STEPS * p + 3)
                for k in range(KC):
                    ins = pe.transpose(proj[:, k * P:(k + 1) * P], xn_next[:, k * P:(k + 1) * P], ident[:])
                ins.then_inc(b_xT, 1)

            def queries(r, cols):
                for k in range(KC):
                    ins = pe.matmul(q_ps[:, 0:2 * QH], xnT_cur[:, k, :], wq_s[:, k, cols],
                                    start=(k == 0), stop=(k == KC - 1))
                ins.then_inc(b_q, 1)

            def queries_t(r):
                pe.wait_ge(b_qs, r + 1)
                for p in range(2):
                    ins = pe.transpose(qT_ps[:, p * P:(p + 1) * P], q_s[:, p * QH:(p + 1) * QH], ident[:])
                ins.then_inc(b_qT, 1)

            def key_scores(r, h):
                pe.wait_ge(b_qTs, r + 1)
                pe.sem_inc(b_gate, 1)
                for p in range(2):
                    ins = pe.matmul(s_ps[:, p * KEYS:(p + 1) * KEYS], qT_s[:, p, :],
                                    keys_s[:, bass.ds(2 * h + p, 1), :].rearrange("p a n -> p (a n)"),
                                    start=True, stop=True)
                ins.then_inc(b_s, 1)

            def head_cols(h):
                return bass.ds(h * (2 * QH), 2 * QH)

            def step(n, kind, h):
                if kind == "last":
                    pe.wait_ge(b_xTs, t_var[0] + 2)
                queries(n + 1, head_cols(h))
                for k in range(TOPK):
                    pe.wait_ge(b_diag, TOPK * n + k + 1)
                    if k == 0 and kind == "first":
                        for b in range(2):
                            pe.matmul(acc[:, HALF[b]], ident[:], h_next[:, HALF[b]], start=True, stop=False)
                    for b in range(2):
                        ins = pe.matmul(acc[:, HALF[b]], diag[:, k % DIAGS, :],
                                        ring[:, k % RING, D + b * 512:D + (b + 1) * 512],
                                        start=False, stop=(kind == "last" and k == TOPK - 1))
                    ins.then_inc(b_free, 1)
                    if k == 1:
                        queries_t(n + 1)
                    if k == 3:
                        key_scores(n + 1, h)
                    if kind == "first" and 4 <= k < 4 + KC:
                        project(t_var[0] + 1, k - 4)
                if kind == "first":
                    transpose_tile(t_var[0] + 1)

            t_var = [0]
            for k in range(KC):
                project(0, k)
            transpose_tile(0)
            pe.wait_ge(b_par, 48)
            pe.wait_ge(b_wq[0], 16)
            pe.wait_ge(b_xTs, 1)
            queries(0, head_cols(0))
            queries_t(0)
            key_scores(0, 0)
            pe.wait_ge(b_wq[1], 16)
            with pe.Fori(0, NT) as t:
                t_var[0] = t
                step(t * PH, "first", 1)
                with pe.Fori(1, PH - 1) as h:
                    step(t * PH + h, "middle", h + 1)
                step(t * PH + (PH - 1), "last", 0)


def program(nc, x, meta, g1, w_in, lam_vecs, sub_g, conv_p, w_out, g2, wq, subkeys_t, table, g_final, out):
    mix_dram = nc.dram_tensor("mix_dram", [NT, P, KC, P], F32, kind="Internal").ap()
    mixer_phase(nc, x, meta, g1, w_in, lam_vecs, sub_g, conv_p, mix_dram)
    expert_phase(nc, x, mix_dram, w_out, g2, wq, subkeys_t, table, g_final, out)


def kernel(**inputs):
    import concourse.bacc as bacc
    import numpy as np
    from concourse.bass_utils import run_bass_kernel_spmd

    a = {k: np.asarray(v) for k, v in inputs.items()}
    arrays = {
        "x": a["x"][0],
        "meta": a["meta_tokens"],
        "g1": a["norm1_g"][0],
        "w_in": a["w_in"][0],
        "lam_vecs": np.concatenate([a["lambda_q1"], a["lambda_k1"], a["lambda_q2"], a["lambda_k2"]], axis=0),
        "sub_g": a["attn_subln_g"][0],
        "conv_p": np.concatenate([a["conv_w"][0], a["conv_b"], a["conv_norm_g"], a["conv_norm_b"]], axis=0).T,
        "w_out": a["w_out"][0],
        "g2": a["norm2_g"][0],
        "wq": a["peer_wq"][0],
        "subkeys_t": a["peer_subkeys"][0].reshape(2 * PH, KEYS, QH).transpose(2, 0, 1),
        "table": np.concatenate([a["peer_u"][0], a["peer_v"][0]], axis=1),
        "g_final": a["final_norm_g"],
    }
    arrays = {k: np.ascontiguousarray(v) for k, v in arrays.items()}
    nc = bacc.Bacc("TRN2", target_bir_lowering=False, num_devices=1)
    args = [nc.dram_tensor(k, v.shape, mybir.dt.from_np(v.dtype), kind="ExternalInput").ap() for k, v in arrays.items()]
    out = nc.dram_tensor("out", (SEQ, D), F32, kind="ExternalOutput").ap()
    program(nc, *args, out)
    result = run_bass_kernel_spmd(nc, [arrays], core_ids=[0])
    return result.results[0]["out"].reshape(1, SEQ, D)
```

```python
import math
from contextlib import ExitStack

import concourse.bass as bass
from concourse import mybir

F32 = mybir.dt.float32
U32 = mybir.dt.uint32
I32 = mybir.dt.int32
ALU = mybir.AluOpType
ACT = mybir.ActivationFunctionType
AX = mybir.AxisListType

P = 128
D = 1024
KC = D // P
SEQ = 1024
NT = SEQ // P
META = 16
POS = META + SEQ
HEADS = 4
COMP = 64
AW = HEADS * 2 * COMP
CG = 4
TAPS = 31
GROUP = 64
IN_COLS = 3 * AW + 2 * CG * P
EPS = 1e-6
LAM_INIT = 0.8 - 0.6 * math.exp(0.0)
SCALE = COMP ** -0.5
SLOPE0 = 2.0 ** (-8.0 / HEADS)
MASKED = -1.0e30
PH = 8
KEYS = 128
TOPK = 16
QH = 128
CAND = TOPK * TOPK
RING = 8
DIAGS = 4
SEGS = [(0, 352), (352, 352), (704, 336)]
NEG = -3.0e38
PIECE_ORDER = (0, 1, 2, 3)


def conv_params_cols():
    return TAPS + 3


def mixer_phase(nc, shared, x, meta, g1, w_in, lam_vecs, sub_g, conv_p, w_out, wq, subkeys_t, mix_dram):
    ctx = ExitStack()
    with ctx:
        def sb(name, shape, dt=F32):
            return ctx.enter_context(nc.sbuf_tensor(name, shape, dt))

        def pb(name, shape):
            return ctx.enter_context(nc.psum_tensor(name, shape, F32))

        def sem(name):
            return ctx.enter_context(nc.semaphore(name))

        ident = sb("identA", [P, P])
        group_mean = sb("group_mean", [P, P])
        g1_cols = sb("g1_cols", [P, KC])
        sub_gain = sb("sub_gain", [P, 1])
        eps_col = sb("eps_col", [P, 1])
        lam_in = sb("lam_in", [P, 4, COMP])
        lam_s = sb("lam_s", [P, 4])
        bias = sb("bias", [P, POS])
        w_out_s = shared["w_out"]
        wv = w_out_s[:, 0:4, :].rearrange("p a (b n) -> p (a b) n", n=AW)
        x_in = w_out_s[:, 4:6, :]
        xn = w_out_s[:, 6:8, :]
        ssum = sb("ssum", [P, 2])
        rstd = sb("rstd", [P, 2])
        xnT = sb("xnT", [P, KC, POS])
        v_all = sb("v_all", [P, NT, AW])
        v_meta = sb("v_meta", [META, AW])
        w_slot = sb("w_slot", [P, 4, KC, P])
        cpar = sb("cpar", [P, CG, conv_params_cols()])
        gate_sig = sb("gate_sig", [P, POS])
        u_next = sb("u_next", [P, POS])
        u_pad = sb("u_pad", [P, TAPS - 1 + POS])
        y = sb("y", [P, SEQ])
        yc = sb("yc", [P, SEQ])
        ysq = sb("ysq", [P, SEQ])
        conv_out = sb("conv_out", [P, SEQ])
        q_next = sb("q_next", [P, POS])
        k_next = sb("k_next", [P, POS])
        qT = sb("qT", [P, SEQ])
        kT = sb("kT", [P, POS])
        dist_i = k_next[:].bitcast(I32)
        z_flat = sb("z", [P, 4 * POS])
        z = z_flat[:].rearrange("p (a c n) -> p a c n", a=2, c=2)
        xnT_tile = z_flat[:, 0:2 * D].rearrange("p (a k n) -> p a k n", a=2, k=KC)
        zmax = sb("zmax", [P, 2, 2, 3])
        nmax = sb("nmax", [P, 2, 2])
        zsum = sb("zsum", [P, 2, 2])
        zinv = sb("zinv", [P, 2, 2])
        aT = sb("aT", [P, 2, 4 * P])
        aT_meta = sb("aT_meta", [META, P])
        o_all = sb("o_all", [P, NT, P])
        o_sq = sb("o_sq", [P, NT, P])
        o_ss = sb("o_ss", [P, NT])
        o_rs = sb("o_rs", [P, NT])
        head_out = sb("head_out", [P, SEQ])

        banks = [pb(f"bankA{i}", [P, 512]) for i in range(8)]

        s_const = sem("a_const")
        s_gate = sem("a_gate")
        s_par = sem("a_par")
        s_lam = sem("a_lam")
        s_x = [sem("a_x0"), sem("a_x1")]
        s_ss = sem("a_ss")
        s_var = sem("a_var")
        s_std = sem("a_std")
        s_rstd = sem("a_rstd")
        s_xn = sem("a_xn")
        s_xT = sem("a_xT")
        s_xTs = sem("a_xTs")
        s_xTall = sem("a_xTall")
        s_wv = sem("a_wv")
        s_v = sem("a_v")
        s_vs = sem("a_vs")
        s_w = [sem(f"a_w{i}") for i in range(4)]
        s_pj = sem("a_pj")
        s_ev = sem("a_ev")
        s_u = sem("a_u")
        s_upad = sem("a_upad")
        s_tap = sem("a_tap")
        s_mean = sem("a_mean")
        s_yc = sem("a_yc")
        s_ysq = sem("a_ysq")
        s_yvar = sem("a_yvar")
        s_ystd = sem("a_ystd")
        s_yrec = sem("a_yrec")
        s_yn = sem("a_yn")
        s_cout = sem("a_cout")
        s_cst = sem("a_cst")
        s_cur = sem("a_cur")
        s_sc = sem("a_sc")
        s_z = sem("a_z")
        s_nm = sem("a_nm")
        s_exp = sem("a_exp")
        s_inv = sem("a_inv")
        s_t1 = sem("a_t1")
        s_a = sem("a_a")
        s_mt = sem("a_mt")
        s_mts = sem("a_mts")
        s_at = sem("a_at")
        s_ats = sem("a_ats")
        s_pv = sem("a_pv")
        s_o = sem("a_o")
        s_fin = sem("a_fin")
        s_ostd = sem("a_ostd")
        s_oT = sem("a_oT")
        s_ho = sem("a_ho")
        s_hst = sem("a_hst")
        s_bias = sem("a_bias")

        block = ctx.enter_context(nc.Block())

        CHUNKS = [-(-(META + P * (i + 1)) // 512) for i in range(NT)]
        GROUPS = [-(-(i + 1) // 4) for i in range(NT)]
        SC_H = 2 * sum(CHUNKS)
        GR_H = sum(GROUPS)
        TAPS_I = -(-TAPS // NT)
        assert SC_H % 2 == 0 and GR_H % 2 == 0

        def chunk(i, n):
            nk = META + P * (i + 1)
            w = -(-nk // CHUNKS[i] // 8) * 8
            return n * w, min(nk, (n + 1) * w)

        def sc_before(i, c):
            return 2 * sum(CHUNKS[:i]) + c * CHUNKS[i]

        def gr_before(i):
            return sum(GROUPS[:i])

        w_in_v = w_in.rearrange("(k p) n -> p k n", p=P)
        x_banks = [banks[0:2], banks[2:4]]
        NM = NT + 1

        def over_tiles(eng, step):
            step(0, 1)
            step(1, 0)
            step(2, 1)
            with eng.Fori(0, (NM - 3) // 2) as j:
                step(2 * j + 3, 0)
                step(2 * j + 4, 1)

        def reused(m):
            return not (isinstance(m, int) and m < 2)

        def rows(m):
            return META if isinstance(m, int) and m == 0 else P

        @block.gpsimd
        def _(pool):
            pool.memset(ident[:], 0.0).then_inc(s_const, 1)
            pool.memset(group_mean[:], 1.0 / GROUP).then_inc(s_const, 1)
            pool.iota(dist_i, [[1, POS]], base=-(META + SEQ - P), channel_multiplier=-1).then_inc(s_const, 1)
            pool.memset(eps_col[:], EPS).then_inc(s_const, 1)
            pool.memset(u_pad[:, 0:TAPS - 1], 0.0).then_inc(s_const, 1)
            pool.wait_ge(s_const, 5)
            pool.affine_select(out=ident[:], in_=ident[:], compare_op=ALU.not_equal, fill=1.0, base=0,
                               pattern=[[-1, P]], channel_multiplier=1).then_inc(s_const, 1)
            pool.affine_select(out=group_mean[:, 0:GROUP], in_=group_mean[:, 0:GROUP], compare_op=ALU.is_ge,
                               fill=0.0, base=GROUP - 1, pattern=[[0, GROUP]],
                               channel_multiplier=-1).then_inc(s_const, 1)
            pool.affine_select(out=group_mean[:, GROUP:P], in_=group_mean[:, GROUP:P], compare_op=ALU.is_ge,
                               fill=0.0, base=-GROUP, pattern=[[0, GROUP]],
                               channel_multiplier=1).then_inc(s_const, 1)
            pool.tensor_copy(bias[:], dist_i).then_inc(s_const, 1)
            pool.wait_ge(s_const, 9)
            pool.affine_select(out=bias[:], in_=bias[:], compare_op=ALU.is_ge, fill=MASKED,
                               base=META + SEQ - P, pattern=[[-1, POS]], channel_multiplier=1).then_inc(s_const, 1)

            def whole(m, slot):
                pool.wait_ge(s_xTs, m + 1)
                pool.sem_inc(s_gate, 1)
                dst = xnT[:, :, 0:META] if rows(m) == META else xnT[:, :, bass.ds((m - 1) * P + META, P)]
                pool.tensor_copy(dst, xnT_tile[:, slot, :, 0:rows(m)]).then_inc(s_xTall, 1)

            over_tiles(pool, whole)

            def current(h):
                pool.wait_ge(s_ev, 9 * h + 6)
                pool.sem_inc(s_gate, 1)
                pool.tensor_copy(qT[:], q_next[:, META:POS]).then_inc(s_cur, 1)
                pool.tensor_copy(kT[:], k_next[:]).then_inc(s_cur, 1)

            def body(r, last):
                for i in range(NT):
                    nk = META + P * (i + 1)
                    pool.wait_ge(s_inv, 2 * (NT * r + i + 1))
                    pool.sem_inc(s_gate, 1)
                    pool.tensor_scalar(z[:, i % 2, 1, 0:nk], z[:, i % 2, 1, 0:nk], zinv[:, i % 2, 1:2], None,
                                       ALU.mult).then_inc(s_t1, 1)
                if not last:
                    pool.wait_ge(s_sc, SC_H * (r + 1))
                    pool.sem_inc(s_gate, 1)
                    current(r + 1)

            current(0)
            with pool.Fori(0, HEADS - 1) as r:
                body(r, False)
            body(HEADS - 1, True)

        @block.sync
        def _(sp):
            def load(m, slot):
                if reused(m):
                    sp.wait_ge(s_xn, m - 1)
                if rows(m) == META:
                    sp.dma_start(x_in[0:META, slot, :], meta).then_inc(s_x[slot], 16)
                    with nc.allow_non_contiguous_dma(reason="small parameter columns"):
                        sp.dma_start(g1_cols[:], g1.rearrange("(k p) -> p k", p=P)).then_inc(s_par, 16)
                        sp.dma_start(sub_gain[:], sub_g.rearrange("(p a) -> p a", a=1)).then_inc(s_par, 16)
                        sp.dma_start(lam_in[:], lam_vecs.rearrange("(o a) b -> o a b", o=1).to_broadcast([P, 4, COMP])
                                     ).then_inc(s_par, 16)
                        sp.dma_start(cpar[:], conv_p.rearrange("(c p) n -> p c n", p=P)).then_inc(s_par, 16)
                else:
                    sp.dma_start(x_in[:, slot, :], x[bass.ds((m - 1) * P, P), :]).then_inc(s_x[slot], 16)
                if isinstance(m, int) and m == 1:
                    sp.dma_start(wv, w_in_v[:, :, 2 * AW:3 * AW]).then_inc(s_wv, 16)

            over_tiles(sp, load)

            def weights(s):
                for slot, at in enumerate((0, AW, 3 * AW + CG * P, 3 * AW)):
                    if not (isinstance(s, int) and s == 0):
                        sp.wait_ge(s_pj, 12 * (s - 1) + 3 * PIECE_ORDER.index(slot) + 3)
                    sp.dma_start(w_slot[:, slot], w_in_v[:, :, bass.ds(s * P + at, P)]).then_inc(s_w[slot], 16)

            def store(r):
                sp.wait_ge(s_cout, r + 1)
                sp.dma_start(mix_dram[:, :, bass.ds(r + HEADS, 1), :].rearrange("t p a n -> p t (a n)"),
                             conv_out[:].rearrange("p (t n) -> p t n", n=P)).then_inc(s_cst, 16)
                sp.wait_ge(s_ho, 2 * (r + 1))
                sp.dma_start(mix_dram[:, :, bass.ds(r, 1), :].rearrange("t p a n -> p t (a n)"),
                             head_out[:].rearrange("p (t n) -> p t n", n=P)).then_inc(s_hst, 16)

            sp.sem_inc(s_cst, 16)
            sp.sem_inc(s_hst, 16)
            weights(0)
            sp.wait_ge(s_v, NM)
            sp.wait_ge(s_xT, NM)
            sp.dma_start(w_out_s[:], w_out.rearrange("(k p) n -> p k n", p=P)).then_inc(shared["w_out_in"], 16)
            sp.dma_start(shared["keys"][:], subkeys_t).then_inc(shared["keys_in"], 16)
            sp.dma_start(shared["wq0"][:], wq.rearrange("(k p) n -> p k n", p=P)[:, :, 0:2 * QH]
                         ).then_inc(shared["wq0_in"], 16)
            weights(1)
            with sp.Fori(0, HEADS - 2) as r:
                weights(r + 2)
                store(r)
            with sp.Fori(HEADS - 2, HEADS) as r:
                store(r)
            sp.wait_ge(s_cst, 16 * (CG + 1))
            sp.wait_ge(s_hst, 16 * (HEADS + 1))

        @block.scalar
        def _(act):
            def values(m, slot):
                act.wait_ge(s_v, m + 1)
                act.sem_inc(s_gate, 1)
                out = v_meta[:] if rows(m) == META else v_all[:, bass.ds(m - 1, 1), :].rearrange("p a n -> p (a n)")
                act.activation(out, banks[4 + slot][0:rows(m), :], ACT.Copy).then_inc(s_vs, 1)

            def norm(m, slot):
                n = rows(m)
                act.wait_ge(s_x[slot], 8 * (m + slot + 1))
                if reused(m):
                    act.wait_ge(s_xT, m - 1)
                act.activation(xn[0:n, slot, :], x_in[0:n, slot, :], ACT.Square,
                               accum_out=ssum[0:n, slot:slot + 1]).then_inc(s_ss, 1)
                act.wait_ge(s_var, m + 1)
                act.activation(ssum[0:n, slot:slot + 1], rstd[0:n, slot:slot + 1], ACT.Sqrt).then_inc(s_std, 1)
                act.wait_ge(s_rstd, m + 1)
                act.activation(xn[0:n, slot, :], x_in[0:n, slot, :], ACT.Copy,
                               scale=rstd[0:n, slot:slot + 1]).then_inc(s_xn, 1)
                if reused(m):
                    values(m - 2, slot)

            over_tiles(act, norm)
            values(NM - 2, 0)
            values(NM - 1, 1)
            act.wait_ge(s_lam, 2)
            act.activation(lam_s[:, 2:4], lam_s[:, 0:2], ACT.Exp).then_inc(s_lam, 1)
            act.wait_ge(s_const, 9)

            def piece_out(s, j):
                slot, n = PIECE_ORDER[j // 3], j % 3
                lo, w = SEGS[n]
                if slot == 0 and n == 0 and not isinstance(s, int):
                    act.wait_ge(s_cur, 2 * s)
                if slot == 2 and n == 0 and not isinstance(s, int):
                    act.wait_ge(s_u, 3 * s)
                act.wait_ge(s_pj, 12 * s + j + 1)
                dst = (q_next, k_next, gate_sig)[slot]
                act.activation(dst[:, lo:lo + w], banks[n][:, 0:w], ACT.Sigmoid if slot == 2 else ACT.Copy
                               ).then_inc(s_ev, 1)

            def gated_in_place(s):
                act.wait_ge(s_u, 3 * (s + 1))
                act.activation(u_pad[:, TAPS - 1:TAPS - 1 + POS], u_next[:], ACT.Copy).then_inc(s_upad, 1)

            def outputs(h, i):
                act.wait_ge(s_mt, NT * h + i + 1)
                act.activation(aT_meta[:], banks[7][0:META, 0:P], ACT.Copy).then_inc(s_mts, 1)
                for g in range(GROUPS[i]):
                    e = gr_before(i) + g
                    nb = min(4, i + 1 - 4 * g)
                    act.wait_ge(s_at, GR_H * h + e + 1)
                    act.activation(aT[:, e % 2, 0:nb * P], banks[5 + e % 2][:, 0:nb * P], ACT.Copy).then_inc(s_ats, 1)
                act.wait_ge(s_pv, NT * h + i + 1)
                if i == 0:
                    act.wait_ge(s_oT, h + 1)
                act.activation(o_all[:, i, :], banks[7][:, P:2 * P], ACT.Copy).then_inc(s_o, 1)

            def body(r, last):
                for i in range(NT):
                    nk = META + P * (i + 1)
                    act.wait_ge(s_nm, 2 * (NT * r + i + 1))
                    for c in range(2):
                        act.activation(z[:, i % 2, c, 0:nk], z[:, i % 2, c, 0:nk], ACT.Exp, scale=SCALE,
                                       bias=nmax[:, i % 2, c:c + 1],
                                       accum_out=zsum[:, i % 2, c:c + 1]).then_inc(s_exp, 1)
                    if not last:
                        piece_out(r + 1, i)
                    if i >= 1:
                        outputs(r, i - 1)
                outputs(r, NT - 1)
                act.wait_ge(s_yc, 2 * (r + 1))
                act.activation(ysq[:], yc[:], ACT.Square).then_inc(s_ysq, 1)
                if not last:
                    piece_out(r + 1, NT)
                act.wait_ge(s_fin, 4 * r + 3)
                act.activation(o_rs[:], o_ss[:], ACT.Sqrt).then_inc(s_ostd, 1)
                act.wait_ge(s_yvar, r + 1)
                for b in range(2):
                    act.activation(ysq[:, b * 512:b * 512 + 512], banks[5 + b][:], ACT.Sqrt,
                                   bias=eps_col[:]).then_inc(s_ystd, 1)
                act.wait_ge(s_yn, r + 1)
                act.sem_inc(s_gate, 1)
                act.wait_ge(s_cst, 16 * (r + 1))
                act.sem_inc(s_gate, 1)
                cp = cpar[:, bass.ds(r, 1), :].rearrange("p a n -> p (a n)")
                act.activation(conv_out[:], yc[:], ACT.Silu, scale=cp[:, TAPS + 1:TAPS + 2],
                               bias=cp[:, TAPS + 2:TAPS + 3]).then_inc(s_cout, 1)
                if not last:
                    gated_in_place(r + 1)

            for j in range(9):
                piece_out(0, j)
            gated_in_place(0)
            with act.Fori(0, HEADS - 1) as r:
                body(r, False)
            body(HEADS - 1, True)

        @block.vector
        def _(dve):
            dve.wait_ge(s_par, 64)

            def tile(m, slot):
                n = rows(m)
                dve.wait_ge(s_ss, m + 1)
                dve.tensor_scalar(rstd[0:n, slot:slot + 1], ssum[0:n, slot:slot + 1], 1.0 / D, EPS, ALU.mult,
                                  ALU.add).then_inc(s_var, 1)
                dve.wait_ge(s_std, m + 1)
                dve.reciprocal(rstd[0:n, slot:slot + 1], ssum[0:n, slot:slot + 1]).then_inc(s_rstd, 1)
                dve.wait_ge(s_xT, m + 1)
                if reused(m):
                    dve.wait_ge(s_v, m - 1)
                    dve.wait_ge(s_xTall, m - 1)
                for b in range(2):
                    ins = dve.tensor_tensor(
                        xnT_tile[:, slot, 4 * b:4 * b + 4, 0:n],
                        x_banks[slot][b][:, 0:4 * P].rearrange("p (k n) -> p k n", n=P)[:, :, 0:n],
                        g1_cols[:, 4 * b:4 * b + 4].unsqueeze(2).to_broadcast([P, 4, n]), ALU.mult)
                ins.then_inc(s_xTs, 1)

            over_tiles(dve, tile)

            for n in range(2):
                dve.tensor_tensor_reduce(lam_in[:, 2 * n, :], lam_in[:, 2 * n, :], lam_in[:, 2 * n + 1, :], 1.0, 0.0,
                                         ALU.mult, ALU.add, lam_s[:, n:n + 1]).then_inc(s_lam, 1)
            dve.wait_ge(s_lam, 3)
            dve.tensor_tensor(lam_s[:, 0:1], lam_s[:, 2:3], lam_s[:, 3:4], ALU.subtract).then_inc(s_lam, 1)
            dve.wait_ge(s_lam, 4)
            dve.tensor_scalar(lam_s[:, 1:2], lam_s[:, 0:1], LAM_INIT, None, ALU.add).then_inc(s_lam, 1)
            dve.tensor_scalar(sub_gain[:], sub_gain[:], 1.0 - LAM_INIT, None, ALU.mult).then_inc(s_lam, 1)
            lam = lam_s[:, 1:2]
            dve.wait_ge(s_const, 10)
            dve.tensor_scalar(bias[:], bias[:], SLOPE0 / SCALE, None, ALU.mult).then_inc(s_bias, 1)

            def gated(s, n):
                lo, w = SEGS[n]
                if n == 0 and not isinstance(s, int):
                    dve.wait_ge(s_upad, s)
                dve.wait_ge(s_pj, 12 * s + 10 + n)
                dve.wait_ge(s_ev, 9 * s + 7 + n)
                dve.tensor_tensor(u_next[:, lo:lo + w], banks[n][:, 0:w], gate_sig[:, lo:lo + w],
                                  ALU.mult).then_inc(s_u, 1)

            def taps(r, i):
                cp = cpar[:, bass.ds(r, 1), :].rearrange("p a n -> p (a n)")
                for k in range(i * TAPS_I, min(TAPS, (i + 1) * TAPS_I)):
                    if k == 0:
                        dve.wait_ge(s_upad, r + 1)
                        dve.tensor_scalar(y[:], u_pad[:, META:META + SEQ], cp[:, 0:1], cp[:, TAPS:TAPS + 1], ALU.mult,
                                          ALU.add).then_inc(s_tap, 1)
                        continue
                    dve.wait_ge(s_tap, TAPS * r + k)
                    dve.scalar_tensor_tensor(out=y[:], in0=u_pad[:, META + k:META + k + SEQ], scalar=cp[:, k:k + 1],
                                             in1=y[:], op0=ALU.mult, op1=ALU.add).then_inc(s_tap, 1)

            def weights(h, i):
                dve.wait_ge(s_exp, 2 * (NT * h + i + 1))
                dve.reciprocal(zinv[:, i % 2, :], zsum[:, i % 2, :]).then_inc(s_inv, 1)
                dve.wait_ge(s_inv, 2 * (NT * h + i) + 1)
                dve.tensor_tensor(zinv[:, i % 2, 1:2], zinv[:, i % 2, 1:2], lam, ALU.mult).then_inc(s_inv, 1)

            def difference(h, i):
                nk = META + P * (i + 1)
                dve.wait_ge(s_t1, NT * h + i + 1)
                dve.scalar_tensor_tensor(out=z[:, i % 2, 0, 0:nk], in0=z[:, i % 2, 0, 0:nk],
                                         scalar=zinv[:, i % 2, 0:1], in1=z[:, i % 2, 1, 0:nk], op0=ALU.mult,
                                         op1=ALU.subtract).then_inc(s_a, 1)

            def body(r, last):
                dve.wait_ge(s_bias, r + 1)
                for i in range(NT):
                    off = (NT - 1 - i) * P
                    if i >= 2:
                        dve.wait_ge(s_at, GR_H * r + gr_before(i - 1))
                        dve.wait_ge(s_mt, NT * r + i - 1)
                    for c in range(2):
                        for n in range(CHUNKS[i]):
                            e = sc_before(i, c) + n
                            lo, hi = chunk(i, n)
                            dve.wait_ge(s_sc, SC_H * r + e + 1)
                            dve.sem_inc(s_gate, 1)
                            dve.tensor_tensor_reduce(z[:, i % 2, c, lo:hi], banks[3 + e % 2][:, 0:hi - lo],
                                                     bias[:, off + lo:off + hi], 1.0, NEG, ALU.add, ALU.max,
                                                     zmax[:, i % 2, c, n:n + 1]).then_inc(s_z, 1)
                    dve.wait_ge(s_z, SC_H * r + sc_before(i + 1, 0) if i + 1 < NT else SC_H * (r + 1))
                    dve.tensor_reduce(nmax[:, i % 2, :], zmax[:, i % 2, :, 0:CHUNKS[i]], AX.X,
                                      ALU.max).then_inc(s_nm, 1)
                    dve.wait_ge(s_nm, 2 * (NT * r + i) + 1)
                    dve.tensor_scalar(nmax[:, i % 2, :], nmax[:, i % 2, :], -SCALE, None, ALU.mult).then_inc(s_nm, 1)
                    if i >= 1:
                        difference(r, i - 1)
                    taps(r, i)
                    weights(r, i)
                difference(r, NT - 1)
                dve.wait_ge(s_mean, r + 1)
                for b in range(2):
                    half = slice(b * 512, b * 512 + 512)
                    dve.tensor_tensor(yc[:, half], y[:, half], banks[5 + b][:], ALU.subtract).then_inc(s_yc, 1)
                dve.wait_ge(s_o, NT * (r + 1))
                dve.tensor_tensor(o_sq[:], o_all[:], o_all[:], ALU.mult).then_inc(s_fin, 1)
                dve.wait_ge(s_fin, 4 * r + 1)
                dve.tensor_reduce(o_ss[:], o_sq[:], AX.X, ALU.add).then_inc(s_fin, 1)
                dve.wait_ge(s_fin, 4 * r + 2)
                dve.tensor_scalar(o_ss[:], o_ss[:], 1.0 / P, EPS, ALU.mult, ALU.add).then_inc(s_fin, 1)
                dve.wait_ge(s_ostd, 2 * r + 1)
                dve.reciprocal(o_rs[:], o_rs[:]).then_inc(s_ostd, 1)
                dve.wait_ge(s_ostd, 2 * r + 2)
                dve.tensor_tensor(o_all[:], o_all[:], o_rs[:].unsqueeze(2).to_broadcast([P, NT, P]),
                                  ALU.mult).then_inc(s_fin, 1)
                dve.wait_ge(s_ystd, 2 * (r + 1))
                dve.reciprocal(ysq[:], ysq[:]).then_inc(s_yrec, 1)
                dve.wait_ge(s_yrec, r + 1)
                dve.tensor_tensor(yc[:], yc[:], ysq[:], ALU.mult).then_inc(s_yn, 1)
                if not last:
                    gated(r + 1, 0)
                dve.wait_ge(s_oT, r + 2)
                dve.wait_ge(s_hst, 16 * (r + 1))
                for b in range(2):
                    dve.tensor_scalar(head_out[:, b * 512:b * 512 + 512], banks[3 + b][:], sub_gain[:], None,
                                      ALU.mult).then_inc(s_ho, 1)
                if not last:
                    gated(r + 1, 1)
                    gated(r + 1, 2)
                    dve.tensor_scalar(bias[:], bias[:], SLOPE0, None, ALU.mult).then_inc(s_bias, 1)
                    dve.wait_ge(s_cout, r + 1)

            for n in range(3):
                gated(0, n)
            with dve.Fori(0, HEADS - 1) as r:
                body(r, False)
            body(HEADS - 1, True)

        @block.tensor
        def _(pe):
            pe.wait_ge(s_const, 10)
            pe.sem_inc(s_oT, 1)

            def values(m, slot):
                n = rows(m)
                if isinstance(m, int) and m == 0:
                    pe.wait_ge(s_wv, 16)
                pe.wait_ge(s_xTs, m + 1)
                if reused(m):
                    pe.wait_ge(s_vs, m - 1)
                for k in range(KC):
                    ins = pe.matmul(banks[4 + slot][0:n, :], xnT_tile[:, slot, k, 0:n], wv[:, k, :],
                                    start=(k == 0), stop=(k == KC - 1))
                ins.then_inc(s_v, 1)

            def tile(m, slot):
                n = rows(m)
                pe.wait_ge(s_xn, m + 1)
                if reused(m):
                    pe.wait_ge(s_xTs, m - 1)
                for k in range(KC):
                    ins = pe.transpose(x_banks[slot][k // 4][:, (k % 4) * P:(k % 4) * P + n],
                                       xn[0:n, slot, k * P:(k + 1) * P], ident[0:n, 0:n])
                ins.then_inc(s_xT, 1)
                if not (isinstance(m, int) and m == 0):
                    values(m - 1, 1 - slot)

            over_tiles(pe, tile)
            values(NM - 1, 1)
            pe.wait_ge(s_xTs, NM)
            pe.wait_ge(s_xTall, NM)

            def piece(s, j):
                slot, n = PIECE_ORDER[j // 3], j % 3
                lo, w = SEGS[n]
                if n == 0:
                    pe.wait_ge(s_w[slot], 16 * (s + 1))
                if j >= 3:
                    pe.wait_ge(s_ev, 9 * s + j - 2)
                elif not (isinstance(s, int) and s == 0):
                    pe.wait_ge(s_u, 3 * (s - 1) + n + 1)
                for k in range(KC):
                    ins = pe.matmul(banks[n][:, 0:w], w_slot[:, slot, k, :], xnT[:, k, lo:lo + w],
                                    start=(k == 0), stop=(k == KC - 1))
                ins.then_inc(s_pj, 1)

            def scores(h, i):
                for c in range(2):
                    for n in range(CHUNKS[i]):
                        e = sc_before(i, c) + n
                        lo, hi = chunk(i, n)
                        if e >= 2:
                            pe.wait_ge(s_z, SC_H * h + e - 1)
                        pe.matmul(banks[3 + e % 2][:, 0:hi - lo], qT[c * COMP:(c + 1) * COMP, i * P:(i + 1) * P],
                                  kT[c * COMP:(c + 1) * COMP, lo:hi], start=True, stop=True).then_inc(s_sc, 1)

            def output(h, i):
                pe.wait_ge(s_a, NT * h + i + 1)
                if i >= 1:
                    pe.wait_ge(s_o, NT * h + i)
                pe.transpose(banks[7][0:META, 0:P], z[:, i % 2, 0, 0:META], ident[:]).then_inc(s_mt, 1)
                for g in range(GROUPS[i]):
                    e = gr_before(i) + g
                    if e >= 2:
                        pe.wait_ge(s_ats, GR_H * h + e - 1)
                    for b in range(4 * g, min(4 * g + 4, i + 1)):
                        ins = pe.transpose(banks[5 + e % 2][:, (b % 4) * P:(b % 4 + 1) * P],
                                           z[:, i % 2, 0, META + b * P:META + (b + 1) * P], ident[:])
                    ins.then_inc(s_at, 1)
                cols = bass.ds(h * P, P)
                pe.wait_ge(s_mts, NT * h + i + 1)
                pe.sem_inc(s_gate, 1)
                pe.matmul(banks[7][:, P:2 * P], aT_meta[:], v_meta[:, cols], start=True, stop=False)
                for g in range(GROUPS[i]):
                    e = gr_before(i) + g
                    pe.wait_ge(s_ats, GR_H * h + e + 1)
                    for b in range(4 * g, min(4 * g + 4, i + 1)):
                        ins = pe.matmul(banks[7][:, P:2 * P], aT[:, e % 2, (b % 4) * P:(b % 4 + 1) * P],
                                        v_all[:, b, cols], start=False, stop=(b == i))
                ins.then_inc(s_pv, 1)

            def body(r, last):
                pe.wait_ge(s_cur, 2 * (r + 1))
                if not isinstance(r, int) or r:
                    pe.wait_ge(s_bias, r + 1)
                for i in range(NT):
                    scores(r, i)
                    if not last:
                        piece(r + 1, i)
                    if i >= 1:
                        output(r, i - 1)
                output(r, NT - 1)
                pe.wait_ge(s_tap, TAPS * (r + 1))
                pe.wait_ge(s_ats, GR_H * (r + 1))
                for b in range(2):
                    ins = pe.matmul(banks[5 + b][:], group_mean[:], y[:, b * 512:b * 512 + 512], start=True, stop=True)
                ins.then_inc(s_mean, 1)
                if not last:
                    piece(r + 1, NT)
                pe.wait_ge(s_ysq, r + 1)
                for b in range(2):
                    ins = pe.matmul(banks[5 + b][:], group_mean[:], ysq[:, b * 512:b * 512 + 512],
                                    start=True, stop=True)
                ins.then_inc(s_yvar, 1)
                if not last:
                    piece(r + 1, NT + 1)
                pe.wait_ge(s_fin, 4 * (r + 1))
                for t in range(NT):
                    ins = pe.transpose(banks[3 + t // 4][:, (t % 4) * P:(t % 4 + 1) * P], o_all[:, t, :], ident[:])
                ins.then_inc(s_oT, 1)
                if not last:
                    piece(r + 1, NT + 2)
                    piece(r + 1, NT + 3)

            for j in range(12):
                piece(0, j)
            with pe.Fori(0, HEADS - 1) as r:
                body(r, False)
            body(HEADS - 1, True)


ROUTE_STEPS = 12
PREP_STEPS = 4
LAST_STEPS = 3


def expert_phase(nc, shared, x, mix_dram, g2, wq, table, g_final, out):
    ctx = ExitStack()
    with ctx:
        def sb(name, shape, dt=F32):
            return ctx.enter_context(nc.sbuf_tensor(name, shape, dt))

        def pb(name, shape):
            return ctx.enter_context(nc.psum_tensor(name, shape, F32))

        def sem(name):
            return ctx.enter_context(nc.semaphore(name))

        ident = sb("identB", [P, P])
        iota_i = sb("iota_i", [P, TOPK], I32)
        iota_f = sb("iota_f", [P, TOPK])
        w_out_s, keys_s, wq_first = shared["w_out"], shared["keys"], shared["wq0"]
        wq_rest = sb("wq_rest", [P, KC, (PH - 1) * 2 * QH])
        g2_row = sb("g2_row", [P, D])
        gf_row = sb("gf_row", [P, D])
        ring = sb("ring", [P, RING, 2 * D])
        mix_t = sb("mix_t", [P, KC, P])
        h_next = sb("h_next", [P, D])
        xn_next = sb("xn_next", [P, D])
        xn_cur = sb("xn_cur", [P, D])
        xnT_cur = sb("xnT_cur", [P, KC, P])
        nrm = sb("nrm", [P, 4])
        q_s = sb("q_s", [P, 2 * QH])
        qT_s = sb("qT_s", [P, 2, P])
        top_v = sb("top_v", [P, 2, TOPK])
        top_i = sb("top_i", [P, 2, TOPK], U32)
        cand = sb("cand", [P, CAND])
        cand_t = sb("cand_t", [P, CAND])
        c_top = sb("c_top", [P, TOPK])
        c_idx = sb("c_idx", [P, TOPK], U32)
        c_ab = sb("c_ab", [P, 2, TOPK], U32)
        hot = sb("hot", [P, 2 * TOPK, TOPK])
        pick = sb("pick", [P, 2, TOPK])
        neg_top = sb("neg_top", [P, 1])
        g_exp = sb("g_exp", [P, TOPK])
        g_sum = sb("g_sum", [P, 2])
        e_next = sb("e_next", [P, TOPK], U32)
        gate_next = sb("gate_next", [P, TOPK])
        e_cur = sb("e_cur", [P, TOPK], U32)
        gate_cur = sb("gate_cur", [P, TOPK])
        dots = sb("dots", [P, TOPK])
        gelu = sb("gelu", [P, TOPK])
        diag = sb("diag", [P, DIAGS, P])

        acc = pb("acc", [P, D])
        proj = pb("projB", [P, D])
        q_ps = pb("q_ps", [P, 512])
        qT_ps = pb("qT_ps", [P, 512])
        s_ps = pb("s_ps", [P, 512])

        b_const = sem("b_const")
        b_gate = sem("b_gate")
        b_par = sem("b_par")
        b_wq = sem("b_wq")
        b_mix = sem("b_mix")
        b_h = sem("b_h")
        b_op = sem("b_op")
        b_hsum = sem("b_hsum")
        b_prep = sem("b_prep")
        b_pss = sem("b_pss")
        b_pstd = sem("b_pstd")
        b_xT = sem("b_xT")
        b_xTs = sem("b_xTs")
        b_q = sem("b_q")
        b_qs = sem("b_qs")
        b_qT = sem("b_qT")
        b_qTs = sem("b_qTs")
        b_s = sem("b_s")
        b_r = sem("b_r")
        b_gexp = sem("b_gexp")
        b_route = sem("b_route")
        b_gates = sem("b_gates")
        b_e = sem("b_e")
        b_row = [sem(f"b_row{r}") for r in range(RING)]
        b_free = sem("b_free")
        b_dot = sem("b_dot")
        b_gelu = sem("b_gelu")
        b_gcur = sem("b_gcur")
        b_diag = sem("b_diag")
        b_lss = sem("b_lss")
        b_lstd = sem("b_lstd")
        b_last = sem("b_last")
        b_out = sem("b_out")

        block = ctx.enter_context(nc.Block())
        wq_v = wq.rearrange("(k p) n -> p k n", p=P)
        HALF = [slice(0, 512), slice(512, 1024)]

        def over_heads(eng, t, step):
            step(t * PH, "first")
            with eng.Fori(1, PH - 1) as h:
                step(t * PH + h, "middle")
            step(t * PH + (PH - 1), "last")

        @block.gpsimd
        def _(pool):
            pool.memset(ident[:], 0.0).then_inc(b_const, 1)
            pool.iota(iota_i[:], [[1, TOPK]], base=0, channel_multiplier=0).then_inc(b_const, 1)
            pool.wait_ge(b_const, 2)
            pool.affine_select(out=ident[:], in_=ident[:], compare_op=ALU.not_equal, fill=1.0, base=0,
                               pattern=[[-1, P]], channel_multiplier=1).then_inc(b_const, 1)
            pool.tensor_copy(iota_f[:], iota_i[:]).then_inc(b_const, 1)

            def step(n, kind):
                pool.wait_ge(b_route, n + 1)
                pool.sem_inc(b_gate, 1)
                for k in range(TOPK):
                    pool.wait_ge(b_free, TOPK * n + k + 1)
                    pool.sem_inc(b_gate, 1)
                    if k % RING == 0:
                        cols = slice(k, k + RING)
                        pool.tensor_copy(e_cur[:, cols], e_next[:, cols]).then_inc(b_e, 1)
                        pool.wait_ge(b_e, TOPK // RING * n + k // RING + 1)
                        pool.sem_inc(b_gate, 1)
                    pool.indirect_dma_start(out=ring[:, k % RING, :], out_offset=None, in_=table[:, :],
                                            in_offset=bass.IndirectOffsetOnAxis(ap=e_cur[:, k:k + 1], axis=0)
                                            ).then_inc(b_row[k % RING], 16)

            with pool.Fori(0, NT) as t:
                over_heads(pool, t, step)

        @block.sync
        def _(sp):
            sp.dma_start(mix_t[:], mix_dram[0, :, :, :]).then_inc(b_mix, 16)
            sp.dma_start(h_next[:], x[0:P, :]).then_inc(b_h, 16)
            sp.dma_start(g2_row[:], g2.rearrange("(a n) -> a n", a=1).to_broadcast([P, D])).then_inc(b_par, 16)
            sp.dma_start(gf_row[:], g_final.rearrange("(a n) -> a n", a=1).to_broadcast([P, D])).then_inc(b_par, 16)
            sp.dma_start(wq_rest[:], wq_v[:, :, 2 * QH:]).then_inc(b_wq, 16)
            sp.sem_inc(b_out, 16)
            with sp.Fori(0, NT) as t:
                nxt = (t + 1) % NT
                sp.wait_ge(b_op, t + 1)
                sp.dma_start(mix_t[:], mix_dram[bass.ds(nxt, 1), :, :, :].rearrange("a p k n -> p (a k) n")
                             ).then_inc(b_mix, 16)
                sp.wait_ge(b_free, PH * TOPK * t + RING + 1)
                sp.dma_start(h_next[:], x[bass.ds(nxt * P, P), :]).then_inc(b_h, 16)
                sp.wait_ge(b_last, LAST_STEPS * (t + 1))
                sp.dma_start(out[bass.ds(t * P, P), :], xn_next[:]).then_inc(b_out, 16)
            sp.wait_ge(b_out, 16 * (NT + 1))
            sp.wait_ge(b_mix, 16 * (NT + 1))
            sp.wait_ge(b_h, 16 * (NT + 1))

        @block.scalar
        def _(act):
            def square_and_root(p):
                act.wait_ge(b_hsum, p + 1)
                if not isinstance(p, int):
                    act.wait_ge(b_out, 16 * p)
                act.activation(xn_next[:], h_next[:], ACT.Square, accum_out=nrm[:, 0:1]).then_inc(b_pss, 1)
                act.wait_ge(b_prep, PREP_STEPS * p + 1)
                act.activation(nrm[:, 0:1], nrm[:, 1:2], ACT.Sqrt).then_inc(b_pstd, 1)

            def transposed(p):
                act.wait_ge(b_xT, p + 1)
                act.activation(xnT_cur[:].rearrange("p k n -> p (k n)"), proj[:], ACT.Copy).then_inc(b_xTs, 1)

            def queries(r):
                act.wait_ge(b_q, r + 1)
                act.activation(q_s[:], q_ps[:, 0:2 * QH], ACT.Copy).then_inc(b_qs, 1)

            def queries_t(r):
                act.wait_ge(b_qT, r + 1)
                act.activation(qT_s[:].rearrange("p a n -> p (a n)"), qT_ps[:, 0:2 * P], ACT.Copy).then_inc(b_qTs, 1)

            def gate_exp(r):
                act.wait_ge(b_r, ROUTE_STEPS * r + 10)
                act.activation(g_exp[:], c_top[:], ACT.Exp, bias=neg_top[:], accum_out=g_sum[:, 0:1]).then_inc(b_gexp, 1)

            def step(n, kind):
                if kind == "last":
                    transposed((n + 1) // PH if isinstance(n, int) else t_var[0] + 1)
                for k in range(TOPK):
                    if k == 1:
                        queries(n + 1)
                    if k == 3:
                        queries_t(n + 1)
                    if k == 9:
                        gate_exp(n + 1)
                    act.wait_ge(b_dot, TOPK * n + k + 1)
                    if k == 0:
                        act.wait_ge(b_gcur, n + 1)
                    act.activation(gelu[:, k:k + 1], dots[:, k:k + 1], ACT.Gelu).then_inc(b_gelu, 1)
                if kind == "first":
                    square_and_root(t_var[0] + 1)

            t_var = [0]
            square_and_root(0)
            transposed(0)
            queries(0)
            queries_t(0)
            gate_exp(0)
            with act.Fori(0, NT) as t:
                t_var[0] = t
                over_heads(act, t, step)
                act.wait_ge(b_free, PH * TOPK * (t + 1) + RING)
                act.wait_ge(b_prep, PREP_STEPS * (t + 2))
                act.activation(xn_next[:], acc[:], ACT.Square, accum_out=nrm[:, 2:3]).then_inc(b_lss, 1)
                act.wait_ge(b_last, LAST_STEPS * t + 1)
                act.activation(nrm[:, 2:3], nrm[:, 3:4], ACT.Sqrt).then_inc(b_lstd, 1)

        @block.vector
        def _(dve):
            dve.wait_ge(b_const, 4)
            dve.wait_ge(b_par, 32)

            def residual(p):
                dve.wait_ge(b_h, 16 * (p + 1))
                dve.wait_ge(b_op, p + 1)
                dve.tensor_tensor(h_next[:], h_next[:], proj[:], ALU.add).then_inc(b_hsum, 1)

            def normalise(p):
                dve.wait_ge(b_pss, p + 1)
                dve.tensor_scalar(nrm[:, 1:2], nrm[:, 0:1], 1.0 / D, EPS, ALU.mult, ALU.add).then_inc(b_prep, 1)
                dve.wait_ge(b_pstd, p + 1)
                dve.reciprocal(nrm[:, 1:2], nrm[:, 0:1]).then_inc(b_prep, 1)
                dve.wait_ge(b_prep, PREP_STEPS * p + 2)
                dve.scalar_tensor_tensor(out=xn_next[:], in0=h_next[:], scalar=nrm[:, 1:2], in1=g2_row[:],
                                         op0=ALU.mult, op1=ALU.mult).then_inc(b_prep, 1)

            def become_current(p):
                dve.wait_ge(b_prep, PREP_STEPS * p + 3)
                dve.wait_ge(b_xT, p + 1)
                dve.tensor_copy(xn_cur[:], xn_next[:]).then_inc(b_prep, 1)

            def after(value):
                dve.wait_ge(b_r, value)
                dve.sem_inc(b_gate, 1)

            def route(r):
                s0 = ROUTE_STEPS * r
                half = [s_ps[:, p * KEYS:(p + 1) * KEYS] for p in range(2)]
                rest = [cand_t[:, p * KEYS:(p + 1) * KEYS] for p in range(2)]
                lo, hi = slice(0, 8), slice(8, TOPK)
                dve.wait_ge(b_s, r + 1)
                dve.sem_inc(b_gate, 1)
                for p in range(2):
                    ins = dve.max(top_v[:, p, lo], half[p])
                ins.then_inc(b_r, 1)
                after(s0 + 1)
                for p in range(2):
                    dve.max_index(top_i[:, p, lo], top_v[:, p, lo], half[p])
                    ins = dve.match_replace(rest[p], top_v[:, p, lo], half[p], NEG)
                ins.then_inc(b_r, 1)
                after(s0 + 2)
                for p in range(2):
                    ins = dve.max(top_v[:, p, hi], rest[p])
                ins.then_inc(b_r, 1)
                after(s0 + 3)
                for p in range(2):
                    dve.max_index(top_i[:, p, hi], top_v[:, p, hi], rest[p])
                dve.tensor_tensor(cand[:].rearrange("p (a b) -> p a b", b=TOPK),
                                  top_v[:, 0, :].unsqueeze(2).to_broadcast([P, TOPK, TOPK]),
                                  top_v[:, 1, :].unsqueeze(1).to_broadcast([P, TOPK, TOPK]), ALU.add).then_inc(b_r, 1)
                after(s0 + 4)
                dve.max(c_top[:, lo], cand[:]).then_inc(b_r, 1)
                after(s0 + 5)
                dve.max_index(c_idx[:, lo], c_top[:, lo], cand[:])
                dve.tensor_scalar(neg_top[:], c_top[:, 0:1], -1.0, None, ALU.mult)
                dve.match_replace(cand_t[:], c_top[:, lo], cand[:], NEG).then_inc(b_r, 1)
                after(s0 + 6)
                dve.max(c_top[:, hi], cand_t[:]).then_inc(b_r, 1)
                after(s0 + 7)
                dve.max_index(c_idx[:, hi], c_top[:, hi], cand_t[:]).then_inc(b_r, 1)
                dve.wait_ge(b_r, s0 + 8)
                dve.tensor_scalar(c_ab[:, 0, :], c_idx[:], 4, None, ALU.logical_shift_right)
                dve.tensor_scalar(c_ab[:, 1, :], c_idx[:], TOPK - 1, None, ALU.bitwise_and).then_inc(b_r, 1)
                dve.wait_ge(b_r, s0 + 9)
                dve.tensor_tensor(hot[:], c_ab[:].rearrange("p a k -> p (a k)").unsqueeze(2).to_broadcast([P, 2 * TOPK, TOPK]),
                                  iota_f[:].unsqueeze(1).to_broadcast([P, 2 * TOPK, TOPK]),
                                  ALU.is_equal).then_inc(b_r, 1)
                dve.wait_ge(b_r, s0 + 10)
                hot4 = hot[:].rearrange("p (a k) j -> p a k j", a=2)
                dve.tensor_tensor(hot4, hot4, top_i[:].unsqueeze(2).to_broadcast([P, 2, TOPK, TOPK]),
                                  ALU.mult).then_inc(b_r, 1)
                dve.wait_ge(b_r, s0 + 11)
                dve.tensor_reduce(pick[:].rearrange("p a k -> p (a k)"), hot[:], AX.X, ALU.add).then_inc(b_r, 1)

            def experts(r):
                dve.wait_ge(b_r, ROUTE_STEPS * (r + 1))
                if not (isinstance(r, int) and r == 0):
                    dve.wait_ge(b_e, TOPK // RING * r)
                dve.scalar_tensor_tensor(out=e_next[:], in0=pick[:, 0, :], scalar=float(KEYS), in1=pick[:, 1, :],
                                         op0=ALU.mult, op1=ALU.add).then_inc(b_route, 1)

            def gates(r):
                dve.wait_ge(b_gexp, r + 1)
                dve.reciprocal(g_sum[:, 1:2], g_sum[:, 0:1]).then_inc(b_gates, 1)
                dve.wait_ge(b_gates, 2 * r + 1)
                dve.tensor_scalar(gate_next[:], g_exp[:], g_sum[:, 1:2], None, ALU.mult).then_inc(b_gates, 1)

            def diagonal(n, k):
                dve.wait_ge(b_gelu, TOPK * n + k + 1)
                dve.wait_ge(b_free, TOPK * n + k + 1 + RING - DIAGS)
                dve.tensor_scalar(diag[:, k % DIAGS, :], ident[:], gelu[:, k:k + 1], gate_cur[:, k:k + 1], ALU.mult,
                                  ALU.mult).then_inc(b_diag, 1)

            def step(n, kind):
                dve.wait_ge(b_gates, 2 * n + 2)
                dve.tensor_copy(gate_cur[:], gate_next[:]).then_inc(b_gcur, 1)
                for k in range(TOPK):
                    dve.wait_ge(b_row[k % RING], 16 * (TOPK // RING * n + k // RING + 1))
                    dve.tensor_tensor_reduce(ring[:, k % RING, 0:D], ring[:, k % RING, 0:D], xn_cur[:], 1.0, 0.0,
                                             ALU.mult, ALU.add, dots[:, k:k + 1]).then_inc(b_dot, 1)
                    if k >= 1:
                        diagonal(n, k - 1)
                    if k == 6:
                        route(n + 1)
                    if k == 11:
                        gates(n + 1)
                    if k == TOPK - RING:
                        experts(n + 1)
                diagonal(n, TOPK - 1)
                dve.wait_ge(b_diag, TOPK * (n + 1))
                dve.sem_inc(b_gate, 1)
                if kind == "first":
                    residual(t_var[0] + 1)
                    normalise(t_var[0] + 1)

            t_var = [0]
            residual(0)
            normalise(0)
            route(0)
            experts(0)
            gates(0)
            become_current(0)
            with dve.Fori(0, NT) as t:
                t_var[0] = t
                dve.wait_ge(b_prep, PREP_STEPS * (t + 1))
                over_heads(dve, t, step)
                become_current(t + 1)
                dve.wait_ge(b_lss, t + 1)
                dve.tensor_scalar(nrm[:, 3:4], nrm[:, 2:3], 1.0 / D, EPS, ALU.mult, ALU.add).then_inc(b_last, 1)
                dve.wait_ge(b_lstd, t + 1)
                dve.reciprocal(nrm[:, 3:4], nrm[:, 2:3]).then_inc(b_last, 1)
                dve.wait_ge(b_last, LAST_STEPS * t + 2)
                dve.scalar_tensor_tensor(out=xn_next[:], in0=acc[:], scalar=nrm[:, 3:4], in1=gf_row[:],
                                         op0=ALU.mult, op1=ALU.mult).then_inc(b_last, 1)

        @block.tensor
        def _(pe):
            pe.wait_ge(b_const, 3)
            pe.wait_ge(shared["w_out_in"], 16)
            pe.sem_inc(b_free, RING)

            def project(p, k):
                if k == 0:
                    pe.wait_ge(b_mix, 16 * (p + 1))
                for b in range(2):
                    ins = pe.matmul(proj[:, HALF[b]], mix_t[:, k, :], w_out_s[:, k, HALF[b]],
                                    start=(k == 0), stop=(k == KC - 1))
                if k == KC - 1:
                    ins.then_inc(b_op, 1)

            def transpose_tile(p):
                pe.wait_ge(b_prep, PREP_STEPS * p + 3)
                for k in range(KC):
                    ins = pe.transpose(proj[:, k * P:(k + 1) * P], xn_next[:, k * P:(k + 1) * P], ident[:])
                ins.then_inc(b_xT, 1)

            def queries(r, h):
                w = wq_first[:, :, :] if isinstance(h, int) and h == 0 else \
                    wq_rest[:, :, bass.ds((h - 1) * (2 * QH), 2 * QH)]
                for k in range(KC):
                    ins = pe.matmul(q_ps[:, 0:2 * QH], xnT_cur[:, k, :], w[:, k, :],
                                    start=(k == 0), stop=(k == KC - 1))
                ins.then_inc(b_q, 1)

            def queries_t(r):
                pe.wait_ge(b_qs, r + 1)
                for p in range(2):
                    ins = pe.transpose(qT_ps[:, p * P:(p + 1) * P], q_s[:, p * QH:(p + 1) * QH], ident[:])
                ins.then_inc(b_qT, 1)

            def key_scores(r, h):
                pe.wait_ge(b_qTs, r + 1)
                pe.sem_inc(b_gate, 1)
                for p in range(2):
                    ins = pe.matmul(s_ps[:, p * KEYS:(p + 1) * KEYS], qT_s[:, p, :],
                                    keys_s[:, bass.ds(2 * h + p, 1), :].rearrange("p a n -> p (a n)"),
                                    start=True, stop=True)
                ins.then_inc(b_s, 1)

            def step(n, kind, h):
                if kind == "last":
                    pe.wait_ge(b_xTs, t_var[0] + 2)
                queries(n + 1, h)
                for k in range(TOPK):
                    pe.wait_ge(b_diag, TOPK * n + k + 1)
                    if k == 0 and kind == "first":
                        for b in range(2):
                            pe.matmul(acc[:, HALF[b]], ident[:], h_next[:, HALF[b]], start=True, stop=False)
                    for b in range(2):
                        ins = pe.matmul(acc[:, HALF[b]], diag[:, k % DIAGS, :],
                                        ring[:, k % RING, D + b * 512:D + (b + 1) * 512],
                                        start=False, stop=(kind == "last" and k == TOPK - 1))
                    ins.then_inc(b_free, 1)
                    if k == 1:
                        queries_t(n + 1)
                    if k == 3:
                        key_scores(n + 1, h)
                    if kind == "first" and 4 <= k < 4 + KC:
                        project(t_var[0] + 1, k - 4)
                if kind == "first":
                    transpose_tile(t_var[0] + 1)

            t_var = [0]
            for k in range(KC):
                project(0, k)
            transpose_tile(0)
            pe.wait_ge(shared["keys_in"], 16)
            pe.wait_ge(shared["wq0_in"], 16)
            pe.wait_ge(b_xTs, 1)
            queries(0, 0)
            queries_t(0)
            key_scores(0, 0)
            pe.wait_ge(b_wq, 16)
            with pe.Fori(0, NT) as t:
                t_var[0] = t
                step(t * PH, "first", 1)
                with pe.Fori(1, PH - 1) as h:
                    step(t * PH + h, "middle", h + 1)
                step(t * PH + (PH - 1), "last", 0)


def program(nc, x, meta, g1, w_in, lam_vecs, sub_g, conv_p, w_out, g2, wq, subkeys_t, table, g_final, out):
    mix_dram = nc.dram_tensor("mix_dram", [NT, P, KC, P], F32, kind="Internal").ap()
    with ExitStack() as ctx:
        shared = {
            "w_out": ctx.enter_context(nc.sbuf_tensor("w_out_s", [P, KC, D], F32)),
            "keys": ctx.enter_context(nc.sbuf_tensor("keys_s", [P, PH * 2, KEYS], F32)),
            "wq0": ctx.enter_context(nc.sbuf_tensor("wq_first", [P, KC, 2 * QH], F32)),
            "w_out_in": ctx.enter_context(nc.semaphore("w_out_in")),
            "keys_in": ctx.enter_context(nc.semaphore("keys_in")),
            "wq0_in": ctx.enter_context(nc.semaphore("wq0_in")),
        }
        mixer_phase(nc, shared, x, meta, g1, w_in, lam_vecs, sub_g, conv_p, w_out, wq, subkeys_t, mix_dram)
        expert_phase(nc, shared, x, mix_dram, g2, wq, table, g_final, out)


def kernel(**inputs):
    import concourse.bacc as bacc
    import numpy as np
    from concourse.bass_utils import run_bass_kernel_spmd

    a = {k: np.asarray(v) for k, v in inputs.items()}
    arrays = {
        "x": a["x"][0],
        "meta": a["meta_tokens"],
        "g1": a["norm1_g"][0],
        "w_in": a["w_in"][0],
        "lam_vecs": np.concatenate([a["lambda_q1"], a["lambda_k1"], a["lambda_q2"], a["lambda_k2"]], axis=0),
        "sub_g": a["attn_subln_g"][0],
        "conv_p": np.concatenate([a["conv_w"][0], a["conv_b"], a["conv_norm_g"], a["conv_norm_b"]], axis=0).T,
        "w_out": a["w_out"][0],
        "g2": a["norm2_g"][0],
        "wq": a["peer_wq"][0],
        "subkeys_t": a["peer_subkeys"][0].reshape(2 * PH, KEYS, QH).transpose(2, 0, 1),
        "table": np.concatenate([a["peer_u"][0], a["peer_v"][0]], axis=1),
        "g_final": a["final_norm_g"],
    }
    arrays = {k: np.ascontiguousarray(v) for k, v in arrays.items()}
    nc = bacc.Bacc("TRN2", target_bir_lowering=False, num_devices=1)
    args = [nc.dram_tensor(k, v.shape, mybir.dt.from_np(v.dtype), kind="ExternalInput").ap() for k, v in arrays.items()]
    out = nc.dram_tensor("out", (SEQ, D), F32, kind="ExternalOutput").ap()
    program(nc, *args, out)
    result = run_bass_kernel_spmd(nc, [arrays], core_ids=[0])
    return result.results[0]["out"].reshape(1, SEQ, D)
```

```python
import math
from contextlib import ExitStack

import concourse.bass as bass
from concourse import mybir

F32 = mybir.dt.float32
U32 = mybir.dt.uint32
I32 = mybir.dt.int32
ALU = mybir.AluOpType
ACT = mybir.ActivationFunctionType
AX = mybir.AxisListType

P = 128
D = 1024
KC = D // P
SEQ = 1024
NT = SEQ // P
META = 16
POS = META + SEQ
HEADS = 4
COMP = 64
AW = HEADS * 2 * COMP
CG = 4
TAPS = 31
GROUP = 64
IN_COLS = 3 * AW + 2 * CG * P
EPS = 1e-6
LAM_INIT = 0.8 - 0.6 * math.exp(0.0)
SCALE = COMP ** -0.5
SLOPE0 = 2.0 ** (-8.0 / HEADS)
MASKED = -1.0e30
PH = 8
KEYS = 128
TOPK = 16
QH = 128
CAND = TOPK * TOPK
RING = 8
DIAGS = 4
SEGS = [(0, 352), (352, 352), (704, 336)]
NEG = -3.0e38


def conv_params_cols():
    return TAPS + 3


def mixer_phase(nc, shared, x, meta, g1, w_in, lam_vecs, sub_g, conv_p, w_out, wq, subkeys_t, mix_dram):
    ctx = ExitStack()
    with ctx:
        def sb(name, shape, dt=F32):
            return ctx.enter_context(nc.sbuf_tensor(name, shape, dt))

        def pb(name, shape):
            return ctx.enter_context(nc.psum_tensor(name, shape, F32))

        def sem(name):
            return ctx.enter_context(nc.semaphore(name))

        ident = sb("identA", [P, P])
        group_mean = sb("group_mean", [P, P])
        g1_cols = sb("g1_cols", [P, KC])
        sub_gain = sb("sub_gain", [P, 1])
        eps_col = sb("eps_col", [P, 1])
        lam_in = sb("lam_in", [P, 4, COMP])
        lam_s = sb("lam_s", [P, 4])
        bias = sb("bias", [P, POS])
        w_out_s = shared["w_out"]
        wv = w_out_s[:, 0:4, :].rearrange("p a (b n) -> p (a b) n", n=AW)
        x_in = w_out_s[:, 4:6, :]
        xn = w_out_s[:, 6:8, :]
        ssum = sb("ssum", [P, 2])
        rstd = sb("rstd", [P, 2])
        xnT = sb("xnT", [P, KC, POS])
        v_all = sb("v_all", [P, NT, AW])
        v_meta = sb("v_meta", [META, AW])
        w_slot = sb("w_slot", [P, 4, KC, P])
        cpar = sb("cpar", [P, CG, conv_params_cols()])
        gate_sig = sb("gate_sig", [P, POS])
        u_next = sb("u_next", [P, POS])
        u_pad = sb("u_pad", [P, TAPS - 1 + POS])
        y = sb("y", [P, SEQ])
        yc = sb("yc", [P, SEQ])
        ysq = sb("ysq", [P, SEQ])
        conv_out = sb("conv_out", [P, SEQ])
        q_next = sb("q_next", [P, POS])
        k_next = sb("k_next", [P, POS])
        qT = sb("qT", [P, SEQ])
        kT = sb("kT", [P, POS])
        dist_i = k_next[:].bitcast(I32)
        z_flat = sb("z", [P, 4 * POS])
        z = z_flat[:].rearrange("p (a c n) -> p a c n", a=2, c=2)
        xnT_tile = z_flat[:, 0:2 * D].rearrange("p (a k n) -> p a k n", a=2, k=KC)
        zmax = sb("zmax", [P, 2, 2, 3])
        nmax = sb("nmax", [P, 2, 2])
        zsum = sb("zsum", [P, 2, 2])
        zinv = sb("zinv", [P, 2, 2])
        aT = sb("aT", [P, 2, 4 * P])
        aT_meta = sb("aT_meta", [META, P])
        o_all = sb("o_all", [P, NT, P])
        o_sq = sb("o_sq", [P, P])
        y_rs = sb("y_rs", [P, 2 * NT])
        no_use = sb("no_use", [P, 1])
        o_ss = sb("o_ss", [P, NT])
        o_rs = sb("o_rs", [P, NT])
        head_out = sb("head_out", [P, SEQ])

        banks = shared["proj"] + [pb(f"bankA{i}", [P, 512]) for i in range(2, 8)]

        s_const = sem("a_const")
        s_gate = sem("a_gate")
        s_par = sem("a_par")
        s_lam = sem("a_lam")
        s_x = [sem("a_x0"), sem("a_x1")]
        s_ss = sem("a_ss")
        s_var = sem("a_var")
        s_std = sem("a_std")
        s_rstd = sem("a_rstd")
        s_xn = sem("a_xn")
        s_xT = sem("a_xT")
        s_xTs = sem("a_xTs")
        s_xTall = sem("a_xTall")
        s_wv = sem("a_wv")
        s_v = sem("a_v")
        s_vs = sem("a_vs")
        s_w = [sem(f"a_w{i}") for i in range(4)]
        s_pj = sem("a_pj")
        s_ev = sem("a_ev")
        s_u = sem("a_u")
        s_upad = sem("a_upad")
        s_tap = sem("a_tap")
        s_mean = sem("a_mean")
        s_yc = sem("a_yc")
        s_ysq = sem("a_ysq")
        s_yvar = sem("a_yvar")
        s_ystd = sem("a_ystd")
        s_yrec = sem("a_yrec")
        s_yb = sem("a_yb")
        s_yf = sem("a_yf")
        s_yn = sem("a_yn")
        s_cout = sem("a_cout")
        s_cst = sem("a_cst")
        s_cur = sem("a_cur")
        s_sc = sem("a_sc")
        s_z = sem("a_z")
        s_nm = sem("a_nm")
        s_exp = sem("a_exp")
        s_inv = sem("a_inv")
        s_a = sem("a_a")
        s_mt = sem("a_mt")
        s_mts = sem("a_mts")
        s_at = sem("a_at")
        s_ats = sem("a_ats")
        s_pv = sem("a_pv")
        s_o = sem("a_o")
        s_mix = sem("a_mix")
        s_fin = sem("a_fin")
        s_ostd = sem("a_ostd")
        s_oT = sem("a_oT")
        s_ho = sem("a_ho")
        s_hst = sem("a_hst")
        s_bias = sem("a_bias")

        block = ctx.enter_context(nc.Block())

        CHUNKS = [-(-(META + P * (i + 1)) // 512) for i in range(NT)]
        GROUPS = [-(-(i + 1) // 4) for i in range(NT)]
        SC_H = 2 * sum(CHUNKS)
        GR_H = sum(GROUPS)
        FACTORS_AT = 3

        def head_banks(r):
            return banks[5:7] if isinstance(r, int) and r == HEADS - 2 else banks[3:5]

        TAPS_TO = [3 * i for i in range(NT + 1)]
        TAPS_TO_6 = [min(TAPS, max(0, 6 * i - 4)) for i in range(NT + 1)]
        assert SC_H % 2 == 0 and GR_H % 2 == 0

        def chunk(i, n):
            nk = META + P * (i + 1)
            w = -(-nk // CHUNKS[i] // 8) * 8
            return n * w, min(nk, (n + 1) * w)

        def sc_before(i):
            return 2 * sum(CHUNKS[:i])

        def gr_before(i):
            return sum(GROUPS[:i])

        w_in_v = w_in.rearrange("(k p) n -> p k n", p=P)
        x_banks = [banks[0:2], banks[2:4]]
        NM = NT + 1

        def over_tiles(eng, step):
            step(0, 1)
            step(1, 0)
            step(2, 1)
            with eng.Fori(0, (NM - 3) // 2) as j:
                step(2 * j + 3, 0)
                step(2 * j + 4, 1)

        def reused(m):
            return not (isinstance(m, int) and m < 2)

        def rows(m):
            return META if isinstance(m, int) and m == 0 else P

        @block.gpsimd
        def _(pool):
            pool.memset(ident[:], 0.0).then_inc(s_const, 1)
            pool.memset(group_mean[:], 1.0 / GROUP).then_inc(s_const, 1)
            pool.iota(dist_i, [[1, POS]], base=-(META + SEQ - P), channel_multiplier=-1).then_inc(s_const, 1)
            pool.memset(eps_col[:], EPS).then_inc(s_const, 1)
            pool.memset(u_pad[:, 0:TAPS - 1], 0.0).then_inc(s_const, 1)
            pool.wait_ge(s_const, 5)
            pool.affine_select(out=ident[:], in_=ident[:], compare_op=ALU.not_equal, fill=1.0, base=0,
                               pattern=[[-1, P]], channel_multiplier=1).then_inc(s_const, 1)
            pool.affine_select(out=group_mean[:, 0:GROUP], in_=group_mean[:, 0:GROUP], compare_op=ALU.is_ge,
                               fill=0.0, base=GROUP - 1, pattern=[[0, GROUP]],
                               channel_multiplier=-1).then_inc(s_const, 1)
            pool.affine_select(out=group_mean[:, GROUP:P], in_=group_mean[:, GROUP:P], compare_op=ALU.is_ge,
                               fill=0.0, base=-GROUP, pattern=[[0, GROUP]],
                               channel_multiplier=1).then_inc(s_const, 1)
            pool.tensor_copy(bias[:], dist_i).then_inc(s_const, 1)
            pool.wait_ge(s_const, 9)
            pool.affine_select(out=bias[:], in_=bias[:], compare_op=ALU.is_ge, fill=MASKED,
                               base=META + SEQ - P, pattern=[[-1, POS]], channel_multiplier=1).then_inc(s_const, 1)

            def whole(m, slot):
                pool.wait_ge(s_xTs, m + 1)
                pool.sem_inc(s_gate, 1)
                dst = xnT[:, :, 0:META] if rows(m) == META else xnT[:, :, bass.ds((m - 1) * P + META, P)]
                pool.tensor_copy(dst, xnT_tile[:, slot, :, 0:rows(m)]).then_inc(s_xTall, 1)

            over_tiles(pool, whole)

            def current(h):
                pool.wait_ge(s_ev, 9 * (h + 1))
                pool.sem_inc(s_gate, 1)
                pool.tensor_copy(qT[:], q_next[:, META:POS]).then_inc(s_cur, 1)
                pool.tensor_copy(kT[:], k_next[:]).then_inc(s_cur, 1)

            def spread_factors(c):
                pool.wait_ge(s_yrec, c + 1)
                pool.sem_inc(s_gate, 1)
                pool.tensor_copy(ysq[:].rearrange("p (a n) -> p a n", n=GROUP),
                                 y_rs[:].unsqueeze(2).to_broadcast([P, 2 * NT, GROUP])).then_inc(s_yb, 1)

            mix_t = shared["mix"]

            def keep_conv(c):
                pool.wait_ge(s_cout, c + 1)
                pool.sem_inc(s_gate, 1)
                pool.tensor_copy(mix_t[:, bass.ds(c + HEADS, 1), :].rearrange("p a n -> p (a n)"),
                                 conv_out[:, 0:P]).then_inc(s_mix, 1)

            def keep_head(r):
                pool.wait_ge(s_ho, 2 * r + 1)
                pool.sem_inc(s_gate, 1)
                pool.tensor_copy(mix_t[:, bass.ds(r, 1), :].rearrange("p a n -> p (a n)"),
                                 head_out[:, 0:P]).then_inc(s_mix, 1)

            pool.sem_inc(s_mix, 2)
            current(0)
            with pool.Fori(0, HEADS - 1) as r:
                spread_factors(r)
                keep_conv(r)
                pool.wait_ge(s_sc, SC_H * (r + 1))
                pool.sem_inc(s_gate, 1)
                current(r + 1)
                keep_head(r)
            spread_factors(HEADS - 1)
            keep_conv(HEADS - 1)
            keep_head(HEADS - 1)

        @block.sync
        def _(sp):
            def load(m, slot):
                if reused(m):
                    sp.wait_ge(s_xn, m - 1)
                if rows(m) == META:
                    sp.dma_start(x_in[0:META, slot, :], meta).then_inc(s_x[slot], 16)
                    with nc.allow_non_contiguous_dma(reason="small parameter columns"):
                        sp.dma_start(g1_cols[:], g1.rearrange("(k p) -> p k", p=P)).then_inc(s_par, 16)
                        sp.dma_start(sub_gain[:], sub_g.rearrange("(p a) -> p a", a=1)).then_inc(s_par, 16)
                        sp.dma_start(lam_in[:], lam_vecs.rearrange("(o a) b -> o a b", o=1).to_broadcast([P, 4, COMP])
                                     ).then_inc(s_par, 16)
                        sp.dma_start(cpar[:], conv_p.rearrange("(c p) n -> p c n", p=P)).then_inc(s_par, 16)
                else:
                    sp.dma_start(x_in[:, slot, :], x[bass.ds((m - 1) * P, P), :]).then_inc(s_x[slot], 16)
                if isinstance(m, int) and m == 1:
                    sp.dma_start(wv, w_in_v[:, :, 2 * AW:3 * AW]).then_inc(s_wv, 16)

            over_tiles(sp, load)

            def weights(s):
                for slot, at, used in ((2, 3 * AW + CG * P, 12 * (s - 1) + 3), (3, 3 * AW, 12 * (s - 1) + 6),
                                       (0, 0, 12 * (s - 1) + 9), (1, AW, 12 * (s - 1) + 12)):
                    if not (isinstance(s, int) and s == 0):
                        sp.wait_ge(s_pj, used)
                        sp.sem_inc(s_gate, 1)
                    sp.dma_start(w_slot[:, slot], w_in_v[:, :, bass.ds(s * P + at, P)]).then_inc(s_w[slot], 16)

            def store_conv(c):
                sp.wait_ge(s_cout, c + 1)
                sp.sem_inc(s_gate, 1)
                sp.dma_start(mix_dram[:, :, bass.ds(c + HEADS, 1), :].rearrange("t p a n -> p t (a n)"),
                             conv_out[:].rearrange("p (t n) -> p t n", n=P)).then_inc(s_cst, 16)

            def store_head(r):
                sp.wait_ge(s_ho, 2 * (r + 1))
                sp.sem_inc(s_gate, 1)
                sp.dma_start(mix_dram[:, :, bass.ds(r, 1), :].rearrange("t p a n -> p t (a n)"),
                             head_out[:].rearrange("p (t n) -> p t n", n=P)).then_inc(s_hst, 16)

            sp.sem_inc(s_cst, 16)
            sp.sem_inc(s_hst, 16)
            weights(0)
            sp.wait_ge(s_v, NM)
            sp.wait_ge(s_xT, NM)
            sp.dma_start(w_out_s[:], w_out.rearrange("(k p) n -> p k n", p=P)).then_inc(shared["w_out_in"], 16)
            sp.dma_start(shared["h"][:], x[0:P, :]).then_inc(shared["h_in"], 16)
            sp.dma_start(shared["keys"][:], subkeys_t).then_inc(shared["keys_in"], 16)
            sp.dma_start(shared["wq0"][:], wq.rearrange("(k p) n -> p k n", p=P)[:, :, 0:2 * QH]
                         ).then_inc(shared["wq0_in"], 16)
            weights(1)
            with sp.Fori(0, HEADS - 2) as r:
                weights(r + 2)
                store_conv(r)
                store_head(r)
            for r in range(HEADS - 2, HEADS):
                store_conv(r)
                store_head(r)
            sp.wait_ge(s_cst, 16 * (CG + 1))
            sp.wait_ge(s_hst, 16 * (HEADS + 1))

        @block.scalar
        def _(act):
            def values(m, slot):
                act.wait_ge(s_v, m + 1)
                act.sem_inc(s_gate, 1)
                out = v_meta[:] if rows(m) == META else v_all[:, bass.ds(m - 1, 1), :].rearrange("p a n -> p (a n)")
                act.activation(out, banks[4 + slot][0:rows(m), :], ACT.Copy).then_inc(s_vs, 1)

            def norm(m, slot):
                n = rows(m)
                act.wait_ge(s_x[slot], 8 * (m + slot + 1))
                if reused(m):
                    act.wait_ge(s_xT, m - 1)
                act.activation(xn[0:n, slot, :], x_in[0:n, slot, :], ACT.Square,
                               accum_out=ssum[0:n, slot:slot + 1]).then_inc(s_ss, 1)
                act.wait_ge(s_var, m + 1)
                act.activation(ssum[0:n, slot:slot + 1], rstd[0:n, slot:slot + 1], ACT.Sqrt).then_inc(s_std, 1)
                act.wait_ge(s_rstd, m + 1)
                act.activation(xn[0:n, slot, :], x_in[0:n, slot, :], ACT.Copy,
                               scale=rstd[0:n, slot:slot + 1]).then_inc(s_xn, 1)
                if reused(m):
                    values(m - 2, slot)

            over_tiles(act, norm)
            values(NM - 2, 0)
            values(NM - 1, 1)
            act.wait_ge(s_lam, 2)
            act.activation(lam_s[:, 2:4], lam_s[:, 0:2], ACT.Exp).then_inc(s_lam, 1)
            act.wait_ge(s_const, 9)

            def head_out_of_psum(s, j):
                lo, w = SEGS[j % 3]
                if j == 0 and not (isinstance(s, int) and s == 0):
                    act.wait_ge(s_cur, 2 * s)
                act.wait_ge(s_pj, 6 * (2 * s + 1) + j + 1)
                dst = q_next if j < 3 else k_next
                act.activation(dst[:, lo:lo + w], banks[j % 3][:, 0:w], ACT.Copy).then_inc(s_ev, 1)

            def gate_out_of_psum(s, n):
                lo, w = SEGS[n]
                if n == 0 and not (isinstance(s, int) and s == 0):
                    act.wait_ge(s_u, 3 * s)
                act.wait_ge(s_pj, 12 * s + n + 1)
                act.activation(gate_sig[:, lo:lo + w], banks[n][:, 0:w], ACT.Sigmoid).then_inc(s_ev, 1)

            def gated_in_place(s):
                act.wait_ge(s_u, 3 * (s + 1))
                act.activation(u_pad[:, TAPS - 1:TAPS - 1 + POS], u_next[:], ACT.Copy).then_inc(s_upad, 1)

            def weights_out_of_psum(h, i):
                act.wait_ge(s_mt, NT * h + i + 1)
                act.activation(aT_meta[:], banks[7][0:META, 0:P], ACT.Copy).then_inc(s_mts, 1)
                for g in range(GROUPS[i]):
                    e = gr_before(i) + g
                    nb = min(4, i + 1 - 4 * g)
                    act.wait_ge(s_at, GR_H * h + e + 1)
                    act.activation(aT[:, e % 2, 0:nb * P], banks[5 + e % 2][:, 0:nb * P], ACT.Copy).then_inc(s_ats, 1)

            def output_out_of_psum(h, i):
                act.wait_ge(s_pv, NT * h + i + 1)
                if i == 0:
                    act.wait_ge(s_oT, h + 1)
                act.activation(o_sq[:], banks[7][:, P:2 * P], ACT.Square, scale=zinv[:, i % 2, 0:1],
                               accum_out=o_ss[:, i:i + 1])
                act.activation(o_all[:, i, :], banks[7][:, P:2 * P], ACT.Copy,
                               scale=zinv[:, i % 2, 0:1]).then_inc(s_o, 1)

            def channel_squares(c):
                act.wait_ge(s_yc, 2 * (c + 1))
                act.activation(ysq[:], yc[:], ACT.Square).then_inc(s_ysq, 1)

            def channel_roots(c):
                act.wait_ge(s_yvar, c + 1)
                act.activation(y_rs[:], banks[0][:, 0:2 * NT], ACT.Sqrt, bias=eps_col[:]).then_inc(s_ystd, 1)

            def channel_output(c):
                act.wait_ge(s_yn, 2 * (c + 1))
                act.sem_inc(s_gate, 1)
                act.wait_ge(s_mix, 2 * c + 1)
                act.sem_inc(s_gate, 1)
                act.wait_ge(s_cst, 16 * (c + 1))
                act.sem_inc(s_gate, 1)
                cp = cpar[:, bass.ds(c, 1), :].rearrange("p a n -> p (a n)")
                act.activation(conv_out[:], yc[:], ACT.Silu, scale=cp[:, TAPS + 1:TAPS + 2],
                               bias=cp[:, TAPS + 2:TAPS + 3]).then_inc(s_cout, 1)

            def body(r, next_head, next_gate):
                for i in range(NT):
                    nk = META + P * (i + 1)
                    if i >= 1:
                        weights_out_of_psum(r, i - 1)
                    act.wait_ge(s_nm, 2 * (NT * r + i + 1))
                    for c in range(2):
                        act.activation(z[:, i % 2, c, 0:nk], z[:, i % 2, c, 0:nk], ACT.Exp, scale=SCALE,
                                       bias=nmax[:, i % 2, c:c + 1],
                                       accum_out=zsum[:, i % 2, c:c + 1]).then_inc(s_exp, 1)
                    if next_head and i < 6:
                        head_out_of_psum(r + 1, i)
                    if next_gate and i >= 6:
                        gate_out_of_psum(r + 2, i - 6)
                    if i >= 1:
                        output_out_of_psum(r, i - 1)
                    if i == 0:
                        channel_squares(r)
                    elif i == 1:
                        channel_roots(r)
                    elif i == FACTORS_AT + 1:
                        channel_output(r)
                weights_out_of_psum(r, NT - 1)
                act.activation(no_use[:], eps_col[:], ACT.Sqrt)
                output_out_of_psum(r, NT - 1)
                act.wait_ge(s_fin, 2 * r + 1)
                act.activation(o_rs[:], o_ss[:], ACT.Sqrt).then_inc(s_ostd, 1)
                if next_gate:
                    gate_out_of_psum(r + 2, 2)
                    gated_in_place(r + 2)

            for n in range(3):
                gate_out_of_psum(0, n)
            gated_in_place(0)
            for j in range(6):
                head_out_of_psum(0, j)
            for n in range(3):
                gate_out_of_psum(1, n)
            gated_in_place(1)
            with act.Fori(0, HEADS - 2) as r:
                body(r, True, True)
            body(HEADS - 2, True, False)
            body(HEADS - 1, False, False)

        @block.vector
        def _(dve):
            dve.wait_ge(s_par, 64)

            def tile(m, slot):
                n = rows(m)
                dve.wait_ge(s_ss, m + 1)
                dve.tensor_scalar(rstd[0:n, slot:slot + 1], ssum[0:n, slot:slot + 1], 1.0 / D, EPS, ALU.mult,
                                  ALU.add).then_inc(s_var, 1)
                dve.wait_ge(s_std, m + 1)
                dve.reciprocal(rstd[0:n, slot:slot + 1], ssum[0:n, slot:slot + 1]).then_inc(s_rstd, 1)
                dve.wait_ge(s_xT, m + 1)
                if reused(m):
                    dve.wait_ge(s_v, m - 1)
                    dve.wait_ge(s_xTall, m - 1)
                for b in range(2):
                    ins = dve.tensor_tensor(
                        xnT_tile[:, slot, 4 * b:4 * b + 4, 0:n],
                        x_banks[slot][b][:, 0:4 * P].rearrange("p (k n) -> p k n", n=P)[:, :, 0:n],
                        g1_cols[:, 4 * b:4 * b + 4].unsqueeze(2).to_broadcast([P, 4, n]), ALU.mult)
                ins.then_inc(s_xTs, 1)

            over_tiles(dve, tile)

            for n in range(2):
                dve.tensor_tensor_reduce(lam_in[:, 2 * n, :], lam_in[:, 2 * n, :], lam_in[:, 2 * n + 1, :], 1.0, 0.0,
                                         ALU.mult, ALU.add, lam_s[:, n:n + 1]).then_inc(s_lam, 1)
            dve.wait_ge(s_lam, 3)
            dve.tensor_tensor(lam_s[:, 0:1], lam_s[:, 2:3], lam_s[:, 3:4], ALU.subtract).then_inc(s_lam, 1)
            dve.wait_ge(s_lam, 4)
            dve.tensor_scalar(lam_s[:, 1:2], lam_s[:, 0:1], -1.0, -LAM_INIT, ALU.mult, ALU.add).then_inc(s_lam, 1)
            dve.tensor_scalar(sub_gain[:], sub_gain[:], 1.0 - LAM_INIT, None, ALU.mult).then_inc(s_lam, 1)
            minus_lam = lam_s[:, 1:2]
            dve.wait_ge(s_const, 10)
            dve.tensor_scalar(bias[:], bias[:], SLOPE0 / SCALE, None, ALU.mult).then_inc(s_bias, 1)

            def gated(s, n):
                lo, w = SEGS[n]
                if n == 0 and not (isinstance(s, int) and s == 0):
                    dve.wait_ge(s_upad, s)
                dve.wait_ge(s_pj, 12 * s + 4 + n)
                dve.wait_ge(s_ev, 9 * s + 1 + n)
                dve.tensor_tensor(u_next[:, lo:lo + w], banks[n][:, 0:w], gate_sig[:, lo:lo + w],
                                  ALU.mult).then_inc(s_u, 1)

            def taps(r, lo, hi):
                cp = cpar[:, bass.ds(r, 1), :].rearrange("p a n -> p (a n)")
                for k in range(lo, hi):
                    if k == 0:
                        dve.wait_ge(s_upad, r + 1)
                        if not (isinstance(r, int) and r == 0):
                            dve.sem_inc(s_gate, 1)
                            dve.wait_ge(s_yc, 2 * r)
                        dve.tensor_scalar(y[:], u_pad[:, META:META + SEQ], cp[:, 0:1], cp[:, TAPS:TAPS + 1], ALU.mult,
                                          ALU.add).then_inc(s_tap, 1)
                        continue
                    dve.wait_ge(s_tap, TAPS * r + k)
                    dve.scalar_tensor_tensor(out=y[:], in0=u_pad[:, META + k:META + k + SEQ], scalar=cp[:, k:k + 1],
                                             in1=y[:], op0=ALU.mult, op1=ALU.add).then_inc(s_tap, 1)

            def weights(h, i):
                dve.wait_ge(s_exp, 2 * (NT * h + i + 1))
                dve.reciprocal(zinv[:, i % 2, :], zsum[:, i % 2, :]).then_inc(s_inv, 1)
                dve.wait_ge(s_inv, 2 * (NT * h + i) + 1)
                dve.scalar_tensor_tensor(out=zinv[:, i % 2, 1:2], in0=zinv[:, i % 2, 1:2], scalar=minus_lam,
                                         in1=zsum[:, i % 2, 0:1], op0=ALU.mult, op1=ALU.mult).then_inc(s_inv, 1)

            def difference(h, i):
                nk = META + P * (i + 1)
                dve.wait_ge(s_inv, 2 * (NT * h + i + 1))
                dve.scalar_tensor_tensor(out=z[:, i % 2, 0, 0:nk], in0=z[:, i % 2, 1, 0:nk],
                                         scalar=zinv[:, i % 2, 1:2], in1=z[:, i % 2, 0, 0:nk], op0=ALU.mult,
                                         op1=ALU.add).then_inc(s_a, 1)

            def centre(c):
                dve.wait_ge(s_mean, c + 1)
                for b in range(2):
                    half = slice(b * 512, b * 512 + 512)
                    dve.tensor_tensor(yc[:, half], y[:, half], banks[1 + b][:], ALU.subtract).then_inc(s_yc, 1)

            def channel_factors(c):
                dve.wait_ge(s_ystd, c + 1)
                dve.reciprocal(y_rs[:], y_rs[:]).then_inc(s_yrec, 1)

            def scale(c):
                dve.wait_ge(s_yf, c + 1)
                for b in range(2):
                    half = slice(b * 512, b * 512 + 512)
                    dve.tensor_tensor(yc[:, half], yc[:, half], banks[1 + b][:], ALU.mult).then_inc(s_yn, 1)

            def head_output(r):
                dve.wait_ge(s_oT, r + 2)
                dve.wait_ge(s_mix, 2 * (r + 1))
                dve.wait_ge(s_hst, 16 * (r + 1))
                for b in range(2):
                    dve.tensor_scalar(head_out[:, b * 512:b * 512 + 512], head_banks(r)[b][:], sub_gain[:], None,
                                      ALU.mult).then_inc(s_ho, 1)

            def body(r, next_head, next_gate):
                upto = TAPS_TO if next_gate else TAPS_TO_6
                dve.wait_ge(s_bias, r + 1)
                for i in range(NT):
                    off = (NT - 1 - i) * P
                    if i >= 2:
                        dve.wait_ge(s_at, GR_H * r + gr_before(i - 1))
                        dve.wait_ge(s_mt, NT * r + i - 1)
                    for n in range(CHUNKS[i]):
                        for c in range(2):
                            e = sc_before(i) + 2 * n + c
                            lo, hi = chunk(i, n)
                            dve.wait_ge(s_sc, SC_H * r + e + 1)
                            dve.sem_inc(s_gate, 1)
                            dve.tensor_tensor_reduce(z[:, i % 2, c, lo:hi], banks[3 + c][:, 0:hi - lo],
                                                     bias[:, off + lo:off + hi], 1.0, NEG, ALU.add, ALU.max,
                                                     zmax[:, i % 2, c, n:n + 1]).then_inc(s_z, 1)
                        if n == 0 and i >= 1:
                            difference(r, i - 1)
                        if n == 0 and i == FACTORS_AT + 1:
                            scale(r)
                    dve.wait_ge(s_z, SC_H * r + sc_before(i + 1))
                    dve.tensor_reduce(nmax[:, i % 2, :], zmax[:, i % 2, :, 0:CHUNKS[i]], AX.X,
                                      ALU.max).then_inc(s_nm, 1)
                    dve.wait_ge(s_nm, 2 * (NT * r + i) + 1)
                    dve.tensor_scalar(nmax[:, i % 2, :], nmax[:, i % 2, :], -SCALE, None, ALU.mult).then_inc(s_nm, 1)
                    if i == 0:
                        centre(r)
                        if not next_head:
                            head_output(r - 1)
                    elif i == 2:
                        channel_factors(r)
                    mid = min(upto[i] + 2, upto[i + 1])
                    if next_head:
                        taps(r + 1, upto[i], mid)
                    weights(r, i)
                    if next_head:
                        taps(r + 1, mid, upto[i + 1])
                difference(r, NT - 1)
                if next_head:
                    taps(r + 1, upto[NT], TAPS)
                dve.wait_ge(s_o, NT * (r + 1))
                dve.tensor_scalar(o_ss[:], o_ss[:], 1.0 / P, EPS, ALU.mult, ALU.add).then_inc(s_fin, 1)
                dve.wait_ge(s_ostd, 2 * r + 1)
                dve.reciprocal(o_rs[:], o_rs[:]).then_inc(s_ostd, 1)
                dve.wait_ge(s_ostd, 2 * r + 2)
                dve.tensor_tensor(o_all[:], o_all[:], o_rs[:].unsqueeze(2).to_broadcast([P, NT, P]),
                                  ALU.mult).then_inc(s_fin, 1)
                if next_gate:
                    gated(r + 2, 0)
                if next_gate or not next_head:
                    head_output(r)
                if next_gate:
                    gated(r + 2, 1)
                    gated(r + 2, 2)
                if next_head:
                    dve.tensor_scalar(bias[:], bias[:], SLOPE0, None, ALU.mult).then_inc(s_bias, 1)
                    dve.wait_ge(s_cout, r + 1)

            for n in range(3):
                gated(0, n)
            taps(0, 0, TAPS)
            for n in range(3):
                gated(1, n)
            with dve.Fori(0, HEADS - 2) as r:
                body(r, True, True)
            body(HEADS - 2, True, False)
            body(HEADS - 1, False, False)

        @block.tensor
        def _(pe):
            pe.wait_ge(s_const, 10)
            pe.sem_inc(s_oT, 1)

            def values(m, slot):
                n = rows(m)
                if isinstance(m, int) and m == 0:
                    pe.wait_ge(s_wv, 16)
                pe.wait_ge(s_xTs, m + 1)
                if reused(m):
                    pe.wait_ge(s_vs, m - 1)
                for k in range(KC):
                    ins = pe.matmul(banks[4 + slot][0:n, :], xnT_tile[:, slot, k, 0:n], wv[:, k, :],
                                    start=(k == 0), stop=(k == KC - 1))
                ins.then_inc(s_v, 1)

            def tile(m, slot):
                n = rows(m)
                pe.wait_ge(s_xn, m + 1)
                if reused(m):
                    pe.wait_ge(s_xTs, m - 1)
                for k in range(KC):
                    ins = pe.transpose(x_banks[slot][k // 4][:, (k % 4) * P:(k % 4) * P + n],
                                       xn[0:n, slot, k * P:(k + 1) * P], ident[0:n, 0:n])
                ins.then_inc(s_xT, 1)
                if not (isinstance(m, int) and m == 0):
                    values(m - 1, 1 - slot)

            over_tiles(pe, tile)
            values(NM - 1, 1)
            pe.wait_ge(s_xTs, NM)
            pe.wait_ge(s_xTall, NM)

            def piece(slot, n, s):
                lo, w = SEGS[n]
                if n == 0:
                    pe.wait_ge(s_w[slot], 16 * (s + 1))
                if slot in (0, 1) and not (isinstance(s, int) and s == 0):
                    if slot == 0 and n >= 1:
                        pe.wait_ge(s_yc, 2 * s)
                    elif slot == 1 and n == 0:
                        pe.wait_ge(s_ystd, s)
                    elif slot == 1:
                        pe.wait_ge(s_yn, 2 * s)
                if slot == 0:
                    pe.wait_ge(s_u, 3 * s + n + 1)
                elif slot == 1:
                    pe.wait_ge(s_ev, 9 * s + n + 4)
                elif slot == 3:
                    pe.wait_ge(s_ev, 9 * s + n + 1)
                elif not (isinstance(s, int) and s == 0):
                    pe.wait_ge(s_ev, 9 * s - 2 + n)
                for k in range(KC):
                    ins = pe.matmul(banks[n][:, 0:w], w_slot[:, slot, k, :], xnT[:, k, lo:lo + w],
                                    start=(k == 0), stop=(k == KC - 1))
                ins.then_inc(s_pj, 1)

            def scores(h, i):
                for n in range(CHUNKS[i]):
                    for c in range(2):
                        e = sc_before(i) + 2 * n + c
                        lo, hi = chunk(i, n)
                        if e >= 2:
                            pe.wait_ge(s_z, SC_H * h + e - 1)
                        pe.matmul(banks[3 + c][:, 0:hi - lo], qT[c * COMP:(c + 1) * COMP, i * P:(i + 1) * P],
                                  kT[c * COMP:(c + 1) * COMP, lo:hi], start=True, stop=True).then_inc(s_sc, 1)

            def transposes(h, i):
                pe.wait_ge(s_a, NT * h + i + 1)
                if i >= 1:
                    pe.wait_ge(s_o, NT * h + i)
                pe.transpose(banks[7][0:META, 0:P], z[:, i % 2, 0, 0:META], ident[:]).then_inc(s_mt, 1)
                for g in range(GROUPS[i]):
                    e = gr_before(i) + g
                    if e >= 2:
                        pe.wait_ge(s_ats, GR_H * h + e - 1)
                    for b in range(4 * g, min(4 * g + 4, i + 1)):
                        ins = pe.transpose(banks[5 + e % 2][:, (b % 4) * P:(b % 4 + 1) * P],
                                           z[:, i % 2, 0, META + b * P:META + (b + 1) * P], ident[:])
                    ins.then_inc(s_at, 1)

            def output(h, i):
                cols = bass.ds(h * P, P)
                pe.wait_ge(s_mts, NT * h + i + 1)
                pe.sem_inc(s_gate, 1)
                pe.matmul(banks[7][:, P:2 * P], aT_meta[:], v_meta[:, cols], start=True, stop=False)
                for g in range(GROUPS[i]):
                    e = gr_before(i) + g
                    pe.wait_ge(s_ats, GR_H * h + e + 1)
                    for b in range(4 * g, min(4 * g + 4, i + 1)):
                        ins = pe.matmul(banks[7][:, P:2 * P], aT[:, e % 2, (b % 4) * P:(b % 4 + 1) * P],
                                        v_all[:, b, cols], start=False, stop=(b == i))
                ins.then_inc(s_pv, 1)

            def group_means(c):
                pe.wait_ge(s_tap, TAPS * (c + 1))
                for b in range(2):
                    ins = pe.matmul(banks[1 + b][:], group_mean[:], y[:, b * 512:b * 512 + 512], start=True, stop=True)
                ins.then_inc(s_mean, 1)

            def group_variances(c):
                pe.wait_ge(s_ysq, c + 1)
                for t in range(NT):
                    ins = pe.matmul(banks[0][:, 2 * t:2 * t + 2], ysq[:, t * P:(t + 1) * P],
                                    group_mean[:, 0:P:GROUP], start=True, stop=True)
                ins.then_inc(s_yvar, 1)

            def group_factors(c):
                pe.wait_ge(s_yb, c + 1)
                for t in range(NT):
                    ins = pe.transpose(banks[1 + t // 4][:, (t % 4) * P:(t % 4 + 1) * P],
                                       ysq[:, t * P:(t + 1) * P], ident[:])
                ins.then_inc(s_yf, 1)

            def transposed_head(r):
                pe.wait_ge(s_fin, 2 * (r + 1))
                for t in range(NT):
                    ins = pe.transpose(head_banks(r)[t // 4][:, (t % 4) * P:(t % 4 + 1) * P], o_all[:, t, :], ident[:])
                ins.then_inc(s_oT, 1)

            def project_tile_0(k):
                pe.wait_ge(s_mix, 2 * k + 4 if k < HEADS else 2 * (k - HEADS) + 3)
                for b in range(2):
                    pe.matmul(banks[b][:], shared["mix"][:, k, :], w_out_s[:, k, b * 512:b * 512 + 512],
                              start=(k == 0), stop=(k == HEADS - 1))

            def body(r, next_head, next_gate):
                pe.wait_ge(s_cur, 2 * (r + 1))
                if next_head and not (isinstance(r, int) and r == 0):
                    pe.wait_ge(s_bias, r + 1)
                elif not next_head:
                    pe.wait_ge(s_z, SC_H * r)
                for i in range(NT):
                    scores(r, i)
                    if i == 0:
                        if next_head:
                            pe.wait_ge(s_u, 3 * (r + 2))
                        else:
                            pe.wait_ge(s_ev, 9 * (r + 1))
                        group_means(r)
                        if not next_head:
                            transposed_head(r - 1)
                    if i == 1 and not next_head:
                        pe.wait_ge(s_ho, 2 * r)
                    if i >= 1:
                        transposes(r, i - 1)
                    if next_head and i < 6:
                        piece(i // 3, i % 3, r + 1)
                    if next_gate and i >= 6:
                        piece(2, i - 6, r + 2)
                    if i == 1:
                        if next_head:
                            pe.wait_ge(s_ev, 9 * (r + 1) + 4)
                        group_variances(r)
                    elif i == FACTORS_AT:
                        if next_head:
                            pe.wait_ge(s_ev, 9 * (r + 1) + 6)
                        group_factors(r)
                    if not next_head and i == 4:
                        pe.wait_ge(s_yn, 2 * CG)
                        pe.wait_ge(shared["w_out_in"], 16)
                    if not next_head and i >= 4:
                        for k in {4: [0, 1, 2], 5: [4, 5], 6: [6], 7: [7]}[i]:
                            project_tile_0(k)
                    if i >= 1:
                        output(r, i - 1)
                transposes(r, NT - 1)
                output(r, NT - 1)
                if next_gate:
                    piece(2, 2, r + 2)
                    piece(3, 0, r + 2)
                if next_gate or not next_head:
                    transposed_head(r)
                if next_gate:
                    piece(3, 1, r + 2)
                    piece(3, 2, r + 2)

            for slot, s in ((2, 0), (3, 0), (0, 0), (1, 0), (2, 1), (3, 1)):
                for n in range(3):
                    piece(slot, n, s)
            with pe.Fori(0, HEADS - 2) as r:
                body(r, True, True)
            body(HEADS - 2, True, False)
            body(HEADS - 1, False, False)
            project_tile_0(HEADS - 1)


ROUTE_STEPS = 12
PREP_STEPS = 4
LAST_STEPS = 3


def expert_phase(nc, shared, x, mix_dram, g2, wq, table, g_final, out):
    ctx = ExitStack()
    with ctx:
        def sb(name, shape, dt=F32):
            return ctx.enter_context(nc.sbuf_tensor(name, shape, dt))

        def pb(name, shape):
            return ctx.enter_context(nc.psum_tensor(name, shape, F32))

        def sem(name):
            return ctx.enter_context(nc.semaphore(name))

        ident = sb("identB", [P, P])
        iota_i = sb("iota_i", [P, TOPK], I32)
        iota_f = sb("iota_f", [P, TOPK])
        w_out_s, keys_s, wq_first = shared["w_out"], shared["keys"], shared["wq0"]
        mix_t, h_next, proj = shared["mix"], shared["h"], shared["proj"]
        wq_rest = sb("wq_rest", [P, KC, (PH - 1) * 2 * QH])
        g2_row = sb("g2_row", [P, D])
        gf_row = sb("gf_row", [P, D])
        ring = sb("ring", [P, RING, 2 * D])
        xn_next = sb("xn_next", [P, D])
        xn_cur = sb("xn_cur", [P, D])
        xnT_cur = sb("xnT_cur", [P, KC, P])
        nrm = sb("nrm", [P, 4])
        q_s = sb("q_s", [P, 2 * QH])
        qT_s = sb("qT_s", [P, 2, P])
        top_v = sb("top_v", [P, 2, TOPK])
        top_i = sb("top_i", [P, 2, TOPK], U32)
        cand = sb("cand", [P, CAND])
        cand_t = sb("cand_t", [P, CAND])
        c_top = sb("c_top", [P, TOPK])
        c_idx = sb("c_idx", [P, TOPK], U32)
        c_ab = sb("c_ab", [P, 2, TOPK], U32)
        hot = sb("hot", [P, 2 * TOPK, TOPK])
        pick = sb("pick", [P, 2, TOPK])
        neg_top = sb("neg_top", [P, 1])
        g_exp = sb("g_exp", [P, TOPK])
        g_sum = sb("g_sum", [P, 2])
        e_next = sb("e_next", [P, TOPK], U32)
        gate_next = sb("gate_next", [P, TOPK])
        e_cur = sb("e_cur", [P, TOPK], U32)
        gate_cur = sb("gate_cur", [P, TOPK])
        dots = sb("dots", [P, TOPK])
        gelu = sb("gelu", [P, TOPK])
        diag = sb("diag", [P, DIAGS, P])

        acc = pb("acc", [P, D])
        q_ps = pb("q_ps", [P, 512])
        qT_ps = pb("qT_ps", [P, 512])
        s_ps = pb("s_ps", [P, 512])

        b_const = sem("b_const")
        b_gate = sem("b_gate")
        b_par = sem("b_par")
        b_wq = sem("b_wq")
        b_mix = sem("b_mix")
        b_h = sem("b_h")
        b_op = sem("b_op")
        b_hsum = sem("b_hsum")
        b_prep = sem("b_prep")
        b_pss = sem("b_pss")
        b_pstd = sem("b_pstd")
        b_xT = sem("b_xT")
        b_xTs = sem("b_xTs")
        b_q = sem("b_q")
        b_qs = sem("b_qs")
        b_qT = sem("b_qT")
        b_qTs = sem("b_qTs")
        b_s = sem("b_s")
        b_r = sem("b_r")
        b_gexp = sem("b_gexp")
        b_route = sem("b_route")
        b_gates = sem("b_gates")
        b_e = sem("b_e")
        b_row = [sem(f"b_row{r}") for r in range(RING)]
        b_free = sem("b_free")
        b_dot = sem("b_dot")
        b_gelu = sem("b_gelu")
        b_gcur = sem("b_gcur")
        b_diag = sem("b_diag")
        b_lss = sem("b_lss")
        b_lstd = sem("b_lstd")
        b_last = sem("b_last")
        b_out = sem("b_out")

        block = ctx.enter_context(nc.Block())
        wq_v = wq.rearrange("(k p) n -> p k n", p=P)
        HALF = [slice(0, 512), slice(512, 1024)]

        def over_heads(eng, t, step):
            step(t * PH, "first")
            with eng.Fori(1, PH - 1) as h:
                step(t * PH + h, "middle")
            step(t * PH + (PH - 1), "last")

        @block.gpsimd
        def _(pool):
            pool.memset(ident[:], 0.0).then_inc(b_const, 1)
            pool.iota(iota_i[:], [[1, TOPK]], base=0, channel_multiplier=0).then_inc(b_const, 1)
            pool.wait_ge(b_const, 2)
            pool.affine_select(out=ident[:], in_=ident[:], compare_op=ALU.not_equal, fill=1.0, base=0,
                               pattern=[[-1, P]], channel_multiplier=1).then_inc(b_const, 1)
            pool.tensor_copy(iota_f[:], iota_i[:]).then_inc(b_const, 1)

            def step(n, kind):
                pool.wait_ge(b_route, n + 1)
                pool.sem_inc(b_gate, 1)
                for k in range(TOPK):
                    pool.wait_ge(b_free, TOPK * n + k + 1)
                    pool.sem_inc(b_gate, 1)
                    if k % RING == 0:
                        cols = slice(k, k + RING)
                        pool.tensor_copy(e_cur[:, cols], e_next[:, cols]).then_inc(b_e, 1)
                        pool.wait_ge(b_e, TOPK // RING * n + k // RING + 1)
                        pool.sem_inc(b_gate, 1)
                    pool.indirect_dma_start(out=ring[:, k % RING, :], out_offset=None, in_=table[:, :],
                                            in_offset=bass.IndirectOffsetOnAxis(ap=e_cur[:, k:k + 1], axis=0)
                                            ).then_inc(b_row[k % RING], 16)

            with pool.Fori(0, NT) as t:
                over_heads(pool, t, step)

        @block.sync
        def _(sp):
            sp.wait_ge(shared["h_in"], 16)
            sp.sem_inc(b_h, 16)
            sp.sem_inc(b_mix, 16)
            sp.dma_start(g2_row[:], g2.rearrange("(a n) -> a n", a=1).to_broadcast([P, D])).then_inc(b_par, 16)
            sp.dma_start(gf_row[:], g_final.rearrange("(a n) -> a n", a=1).to_broadcast([P, D])).then_inc(b_par, 16)
            sp.dma_start(wq_rest[:], wq_v[:, :, 2 * QH:]).then_inc(b_wq, 16)
            sp.sem_inc(b_out, 16)
            with sp.Fori(0, NT) as t:
                nxt = (t + 1) % NT
                sp.wait_ge(b_op, t + 1)
                sp.dma_start(mix_t[:], mix_dram[bass.ds(nxt, 1), :, :, :].rearrange("a p k n -> p (a k) n")
                             ).then_inc(b_mix, 16)
                sp.wait_ge(b_free, PH * TOPK * t + RING + 1)
                sp.dma_start(h_next[:], x[bass.ds(nxt * P, P), :]).then_inc(b_h, 16)
                sp.wait_ge(b_last, LAST_STEPS * (t + 1))
                sp.dma_start(out[bass.ds(t * P, P), :], xn_next[:]).then_inc(b_out, 16)
            sp.wait_ge(b_out, 16 * (NT + 1))
            sp.wait_ge(b_mix, 16 * (NT + 1))
            sp.wait_ge(b_h, 16 * (NT + 1))

        @block.scalar
        def _(act):
            def square_and_root(p):
                act.wait_ge(b_hsum, p + 1)
                if not isinstance(p, int):
                    act.wait_ge(b_out, 16 * p)
                act.activation(xn_next[:], h_next[:], ACT.Square, accum_out=nrm[:, 0:1]).then_inc(b_pss, 1)
                act.wait_ge(b_prep, PREP_STEPS * p + 1)
                act.activation(nrm[:, 0:1], nrm[:, 1:2], ACT.Sqrt).then_inc(b_pstd, 1)

            def transposed(p):
                act.wait_ge(b_xT, p + 1)
                for b in range(2):
                    ins = act.activation(xnT_cur[:, 4 * b:4 * b + 4, :].rearrange("p k n -> p (k n)"), proj[b][:],
                                         ACT.Copy)
                ins.then_inc(b_xTs, 1)

            def queries(r):
                act.wait_ge(b_q, r + 1)
                act.activation(q_s[:], q_ps[:, 0:2 * QH], ACT.Copy).then_inc(b_qs, 1)

            def queries_t(r):
                act.wait_ge(b_qT, r + 1)
                act.activation(qT_s[:].rearrange("p a n -> p (a n)"), qT_ps[:, 0:2 * P], ACT.Copy).then_inc(b_qTs, 1)

            def gate_exp(r):
                act.wait_ge(b_r, ROUTE_STEPS * r + 10)
                act.activation(g_exp[:], c_top[:], ACT.Exp, bias=neg_top[:], accum_out=g_sum[:, 0:1]).then_inc(b_gexp, 1)

            def step(n, kind):
                if kind == "last":
                    transposed((n + 1) // PH if isinstance(n, int) else t_var[0] + 1)
                for k in range(TOPK):
                    if k == 1:
                        queries(n + 1)
                    if k == 3:
                        queries_t(n + 1)
                    if k == 9:
                        gate_exp(n + 1)
                    act.wait_ge(b_dot, TOPK * n + k + 1)
                    if k == 0:
                        act.wait_ge(b_gcur, n + 1)
                    act.activation(gelu[:, k:k + 1], dots[:, k:k + 1], ACT.Gelu).then_inc(b_gelu, 1)
                if kind == "first":
                    square_and_root(t_var[0] + 1)

            t_var = [0]
            square_and_root(0)
            transposed(0)
            queries(0)
            queries_t(0)
            gate_exp(0)
            with act.Fori(0, NT) as t:
                t_var[0] = t
                over_heads(act, t, step)
                act.wait_ge(b_free, PH * TOPK * (t + 1) + RING)
                act.wait_ge(b_prep, PREP_STEPS * (t + 2))
                act.activation(xn_next[:], acc[:], ACT.Square, accum_out=nrm[:, 2:3]).then_inc(b_lss, 1)
                act.wait_ge(b_last, LAST_STEPS * t + 1)
                act.activation(nrm[:, 2:3], nrm[:, 3:4], ACT.Sqrt).then_inc(b_lstd, 1)

        @block.vector
        def _(dve):
            dve.wait_ge(b_const, 4)

            def residual(p):
                dve.wait_ge(b_h, 16 * (p + 1))
                dve.wait_ge(b_op, p + 1)
                for b in range(2):
                    ins = dve.tensor_tensor(h_next[:, HALF[b]], h_next[:, HALF[b]], proj[b][:], ALU.add)
                ins.then_inc(b_hsum, 1)

            def normalise(p):
                dve.wait_ge(b_pss, p + 1)
                dve.tensor_scalar(nrm[:, 1:2], nrm[:, 0:1], 1.0 / D, EPS, ALU.mult, ALU.add).then_inc(b_prep, 1)
                dve.wait_ge(b_pstd, p + 1)
                dve.reciprocal(nrm[:, 1:2], nrm[:, 0:1]).then_inc(b_prep, 1)
                dve.wait_ge(b_prep, PREP_STEPS * p + 2)
                dve.scalar_tensor_tensor(out=xn_next[:], in0=h_next[:], scalar=nrm[:, 1:2], in1=g2_row[:],
                                         op0=ALU.mult, op1=ALU.mult).then_inc(b_prep, 1)

            def become_current(p):
                dve.wait_ge(b_prep, PREP_STEPS * p + 3)
                dve.wait_ge(b_xT, p + 1)
                dve.tensor_copy(xn_cur[:], xn_next[:]).then_inc(b_prep, 1)

            def after(value):
                dve.wait_ge(b_r, value)
                dve.sem_inc(b_gate, 1)

            def route(r):
                s0 = ROUTE_STEPS * r
                half = [s_ps[:, p * KEYS:(p + 1) * KEYS] for p in range(2)]
                rest = [cand_t[:, p * KEYS:(p + 1) * KEYS] for p in range(2)]
                lo, hi = slice(0, 8), slice(8, TOPK)
                dve.wait_ge(b_s, r + 1)
                dve.sem_inc(b_gate, 1)
                for p in range(2):
                    ins = dve.max(top_v[:, p, lo], half[p])
                ins.then_inc(b_r, 1)
                after(s0 + 1)
                for p in range(2):
                    dve.max_index(top_i[:, p, lo], top_v[:, p, lo], half[p])
                    ins = dve.match_replace(rest[p], top_v[:, p, lo], half[p], NEG)
                ins.then_inc(b_r, 1)
                after(s0 + 2)
                for p in range(2):
                    ins = dve.max(top_v[:, p, hi], rest[p])
                ins.then_inc(b_r, 1)
                after(s0 + 3)
                for p in range(2):
                    dve.max_index(top_i[:, p, hi], top_v[:, p, hi], rest[p])
                dve.tensor_tensor(cand[:].rearrange("p (a b) -> p a b", b=TOPK),
                                  top_v[:, 0, :].unsqueeze(2).to_broadcast([P, TOPK, TOPK]),
                                  top_v[:, 1, :].unsqueeze(1).to_broadcast([P, TOPK, TOPK]), ALU.add).then_inc(b_r, 1)
                after(s0 + 4)
                dve.max(c_top[:, lo], cand[:]).then_inc(b_r, 1)
                after(s0 + 5)
                dve.max_index(c_idx[:, lo], c_top[:, lo], cand[:])
                dve.tensor_scalar(neg_top[:], c_top[:, 0:1], -1.0, None, ALU.mult)
                dve.match_replace(cand_t[:], c_top[:, lo], cand[:], NEG).then_inc(b_r, 1)
                after(s0 + 6)
                dve.max(c_top[:, hi], cand_t[:]).then_inc(b_r, 1)
                after(s0 + 7)
                dve.max_index(c_idx[:, hi], c_top[:, hi], cand_t[:]).then_inc(b_r, 1)
                dve.wait_ge(b_r, s0 + 8)
                dve.tensor_scalar(c_ab[:, 0, :], c_idx[:], 4, None, ALU.logical_shift_right)
                dve.tensor_scalar(c_ab[:, 1, :], c_idx[:], TOPK - 1, None, ALU.bitwise_and).then_inc(b_r, 1)
                dve.wait_ge(b_r, s0 + 9)
                dve.tensor_tensor(hot[:], c_ab[:].rearrange("p a k -> p (a k)").unsqueeze(2).to_broadcast([P, 2 * TOPK, TOPK]),
                                  iota_f[:].unsqueeze(1).to_broadcast([P, 2 * TOPK, TOPK]),
                                  ALU.is_equal).then_inc(b_r, 1)
                dve.wait_ge(b_r, s0 + 10)
                hot4 = hot[:].rearrange("p (a k) j -> p a k j", a=2)
                dve.tensor_tensor(hot4, hot4, top_i[:].unsqueeze(2).to_broadcast([P, 2, TOPK, TOPK]),
                                  ALU.mult).then_inc(b_r, 1)
                dve.wait_ge(b_r, s0 + 11)
                dve.tensor_reduce(pick[:].rearrange("p a k -> p (a k)"), hot[:], AX.X, ALU.add).then_inc(b_r, 1)

            def experts(r):
                dve.wait_ge(b_r, ROUTE_STEPS * (r + 1))
                if not (isinstance(r, int) and r == 0):
                    dve.wait_ge(b_e, TOPK // RING * r)
                dve.scalar_tensor_tensor(out=e_next[:], in0=pick[:, 0, :], scalar=float(KEYS), in1=pick[:, 1, :],
                                         op0=ALU.mult, op1=ALU.add).then_inc(b_route, 1)

            def gates(r):
                dve.wait_ge(b_gexp, r + 1)
                dve.reciprocal(g_sum[:, 1:2], g_sum[:, 0:1]).then_inc(b_gates, 1)
                dve.wait_ge(b_gates, 2 * r + 1)
                dve.tensor_scalar(gate_next[:], g_exp[:], g_sum[:, 1:2], None, ALU.mult).then_inc(b_gates, 1)

            def diagonal(n, k):
                dve.wait_ge(b_gelu, TOPK * n + k + 1)
                dve.wait_ge(b_free, TOPK * n + k + 1 + RING - DIAGS)
                dve.tensor_scalar(diag[:, k % DIAGS, :], ident[:], gelu[:, k:k + 1], gate_cur[:, k:k + 1], ALU.mult,
                                  ALU.mult).then_inc(b_diag, 1)

            def step(n, kind):
                dve.wait_ge(b_gates, 2 * n + 2)
                dve.tensor_copy(gate_cur[:], gate_next[:]).then_inc(b_gcur, 1)
                for k in range(TOPK):
                    dve.wait_ge(b_row[k % RING], 16 * (TOPK // RING * n + k // RING + 1))
                    dve.tensor_tensor_reduce(ring[:, k % RING, 0:D], ring[:, k % RING, 0:D], xn_cur[:], 1.0, 0.0,
                                             ALU.mult, ALU.add, dots[:, k:k + 1]).then_inc(b_dot, 1)
                    if k >= 1:
                        diagonal(n, k - 1)
                    if k == 6:
                        route(n + 1)
                    if k == 11:
                        gates(n + 1)
                    if k == TOPK - RING:
                        experts(n + 1)
                diagonal(n, TOPK - 1)
                dve.wait_ge(b_diag, TOPK * (n + 1))
                dve.sem_inc(b_gate, 1)
                if kind == "first":
                    residual(t_var[0] + 1)
                    normalise(t_var[0] + 1)

            t_var = [0]
            residual(0)
            dve.wait_ge(b_par, 32)
            normalise(0)
            route(0)
            experts(0)
            gates(0)
            become_current(0)
            with dve.Fori(0, NT) as t:
                t_var[0] = t
                dve.wait_ge(b_prep, PREP_STEPS * (t + 1))
                over_heads(dve, t, step)
                become_current(t + 1)
                dve.wait_ge(b_lss, t + 1)
                dve.tensor_scalar(nrm[:, 3:4], nrm[:, 2:3], 1.0 / D, EPS, ALU.mult, ALU.add).then_inc(b_last, 1)
                dve.wait_ge(b_lstd, t + 1)
                dve.reciprocal(nrm[:, 3:4], nrm[:, 2:3]).then_inc(b_last, 1)
                dve.wait_ge(b_last, LAST_STEPS * t + 2)
                dve.scalar_tensor_tensor(out=xn_next[:], in0=acc[:], scalar=nrm[:, 3:4], in1=gf_row[:],
                                         op0=ALU.mult, op1=ALU.mult).then_inc(b_last, 1)

        @block.tensor
        def _(pe):
            pe.wait_ge(b_const, 3)
            pe.sem_inc(b_op, 1)
            pe.sem_inc(b_free, RING)

            def project(p, k):
                if k == 0:
                    pe.wait_ge(b_mix, 16 * (p + 1))
                for b in range(2):
                    ins = pe.matmul(proj[b][:], mix_t[:, k, :], w_out_s[:, k, HALF[b]],
                                    start=(k == 0), stop=(k == KC - 1))
                if k == KC - 1:
                    ins.then_inc(b_op, 1)

            def transpose_tile(p):
                pe.wait_ge(b_prep, PREP_STEPS * p + 3)
                for k in range(KC):
                    ins = pe.transpose(proj[k // 4][:, (k % 4) * P:(k % 4 + 1) * P], xn_next[:, k * P:(k + 1) * P], ident[:])
                ins.then_inc(b_xT, 1)

            def queries(r, h):
                w = wq_first[:, :, :] if isinstance(h, int) and h == 0 else \
                    wq_rest[:, :, bass.ds((h - 1) * (2 * QH), 2 * QH)]
                for k in range(KC):
                    ins = pe.matmul(q_ps[:, 0:2 * QH], xnT_cur[:, k, :], w[:, k, :],
                                    start=(k == 0), stop=(k == KC - 1))
                ins.then_inc(b_q, 1)

            def queries_t(r):
                pe.wait_ge(b_qs, r + 1)
                for p in range(2):
                    ins = pe.transpose(qT_ps[:, p * P:(p + 1) * P], q_s[:, p * QH:(p + 1) * QH], ident[:])
                ins.then_inc(b_qT, 1)

            def key_scores(r, h):
                pe.wait_ge(b_qTs, r + 1)
                pe.sem_inc(b_gate, 1)
                for p in range(2):
                    ins = pe.matmul(s_ps[:, p * KEYS:(p + 1) * KEYS], qT_s[:, p, :],
                                    keys_s[:, bass.ds(2 * h + p, 1), :].rearrange("p a n -> p (a n)"),
                                    start=True, stop=True)
                ins.then_inc(b_s, 1)

            def step(n, kind, h):
                if kind == "last":
                    pe.wait_ge(b_xTs, t_var[0] + 2)
                queries(n + 1, h)
                for k in range(TOPK):
                    pe.wait_ge(b_diag, TOPK * n + k + 1)
                    if k == 0 and kind == "first":
                        for b in range(2):
                            pe.matmul(acc[:, HALF[b]], ident[:], h_next[:, HALF[b]], start=True, stop=False)
                    for b in range(2):
                        ins = pe.matmul(acc[:, HALF[b]], diag[:, k % DIAGS, :],
                                        ring[:, k % RING, D + b * 512:D + (b + 1) * 512],
                                        start=False, stop=(kind == "last" and k == TOPK - 1))
                    ins.then_inc(b_free, 1)
                    if k == 1:
                        queries_t(n + 1)
                    if k == 3:
                        key_scores(n + 1, h)
                    if kind == "first" and 4 <= k < 4 + KC:
                        project(t_var[0] + 1, k - 4)
                if kind == "first":
                    transpose_tile(t_var[0] + 1)

            t_var = [0]
            transpose_tile(0)
            pe.wait_ge(shared["keys_in"], 16)
            pe.wait_ge(shared["wq0_in"], 16)
            pe.wait_ge(b_xTs, 1)
            queries(0, 0)
            queries_t(0)
            key_scores(0, 0)
            pe.wait_ge(b_wq, 16)
            with pe.Fori(0, NT) as t:
                t_var[0] = t
                step(t * PH, "first", 1)
                with pe.Fori(1, PH - 1) as h:
                    step(t * PH + h, "middle", h + 1)
                step(t * PH + (PH - 1), "last", 0)


def program(nc, x, meta, g1, w_in, lam_vecs, sub_g, conv_p, w_out, g2, wq, subkeys_t, table, g_final, out):
    mix_dram = nc.dram_tensor("mix_dram", [NT, P, KC, P], F32, kind="Internal").ap()
    with ExitStack() as ctx:
        shared = {
            "w_out": ctx.enter_context(nc.sbuf_tensor("w_out_s", [P, KC, D], F32)),
            "keys": ctx.enter_context(nc.sbuf_tensor("keys_s", [P, PH * 2, KEYS], F32)),
            "wq0": ctx.enter_context(nc.sbuf_tensor("wq_first", [P, KC, 2 * QH], F32)),
            "mix": ctx.enter_context(nc.sbuf_tensor("mix_t", [P, KC, P], F32)),
            "h": ctx.enter_context(nc.sbuf_tensor("h_next", [P, D], F32)),
            "proj": [ctx.enter_context(nc.psum_tensor(f"proj{b}", [P, 512], F32)) for b in range(2)],
            "h_in": ctx.enter_context(nc.semaphore("h_in")),
            "w_out_in": ctx.enter_context(nc.semaphore("w_out_in")),
            "keys_in": ctx.enter_context(nc.semaphore("keys_in")),
            "wq0_in": ctx.enter_context(nc.semaphore("wq0_in")),
        }
        mixer_phase(nc, shared, x, meta, g1, w_in, lam_vecs, sub_g, conv_p, w_out, wq, subkeys_t, mix_dram)
        expert_phase(nc, shared, x, mix_dram, g2, wq, table, g_final, out)


def kernel(**inputs):
    import concourse.bacc as bacc
    import numpy as np
    from concourse.bass_utils import run_bass_kernel_spmd

    a = {k: np.asarray(v) for k, v in inputs.items()}
    arrays = {
        "x": a["x"][0],
        "meta": a["meta_tokens"],
        "g1": a["norm1_g"][0],
        "w_in": a["w_in"][0],
        "lam_vecs": np.concatenate([a["lambda_q1"], a["lambda_k1"], a["lambda_q2"], a["lambda_k2"]], axis=0),
        "sub_g": a["attn_subln_g"][0],
        "conv_p": np.concatenate([a["conv_w"][0], a["conv_b"], a["conv_norm_g"], a["conv_norm_b"]], axis=0).T,
        "w_out": a["w_out"][0],
        "g2": a["norm2_g"][0],
        "wq": a["peer_wq"][0],
        "subkeys_t": a["peer_subkeys"][0].reshape(2 * PH, KEYS, QH).transpose(2, 0, 1),
        "table": np.concatenate([a["peer_u"][0], a["peer_v"][0]], axis=1),
        "g_final": a["final_norm_g"],
    }
    arrays = {k: np.ascontiguousarray(v) for k, v in arrays.items()}
    nc = bacc.Bacc("TRN2", target_bir_lowering=False, num_devices=1)
    args = [nc.dram_tensor(k, v.shape, mybir.dt.from_np(v.dtype), kind="ExternalInput").ap() for k, v in arrays.items()]
    out = nc.dram_tensor("out", (SEQ, D), F32, kind="ExternalOutput").ap()
    program(nc, *args, out)
    result = run_bass_kernel_spmd(nc, [arrays], core_ids=[0])
    return result.results[0]["out"].reshape(1, SEQ, D)
```
